# Optimizing a Trainium2 kernel written in Bass

```python
import jax, jax.numpy as jnp
from jax import lax
import numpy as np

D_MODEL = 1024
BATCH = 1
SEQ = 256
DEPTH = 2

N_A_LAYERS = DEPTH // 2
N_B_LAYERS = DEPTH - N_A_LAYERS
CONV_WIDTH = 3
D_FF = ((8 * D_MODEL // 3 + 127) // 128) * 128
HEAD_DIM = 128
N_HEADS = D_MODEL // HEAD_DIM
BLOCK_SIZE = 256
TOP_K_BLOCKS = 3
Q_CHUNK = 128
EPS = 1e-6

kernel_name = "yoco_shortconv_moba_convffn"

def rmsnorm(x, g):
    xf = x.astype(jnp.float32)
    y = xf * lax.rsqrt(jnp.mean(xf * xf, axis=-1, keepdims=True) + EPS)
    return (y * g.astype(jnp.float32)).astype(x.dtype)

def causal_dwconv(x, w):
    c = x.shape[-1]
    return lax.conv_general_dilated(
        x, w[:, None, :].astype(x.dtype), window_strides=(1,),
        padding=[(CONV_WIDTH - 1, 0)], dimension_numbers=("NWC", "WIO", "NWC"),
        feature_group_count=c)

def short_conv_mixer(h, w_in, w_conv, w_out):
    bg, cg, xv = jnp.split(h @ w_in, 3, axis=-1)
    return (bg * causal_dwconv(cg * xv, w_conv)) @ w_out

def conv_ffn(h, w_up, w_conv, b_conv, w_down):
    g, u = jnp.split(h @ w_up, 2, axis=-1)
    g = causal_dwconv(g, w_conv) + b_conv.astype(h.dtype)
    return (jax.nn.silu(g) * u) @ w_down

def alibi_slopes(n_heads):
    return jnp.asarray([2.0 ** (-8.0 * (i + 1) / n_heads) for i in range(n_heads)], dtype=jnp.float32)

def shared_kv(x, kv_norm, w_kv):
    b, s, _ = x.shape
    h = rmsnorm(x, kv_norm)
    k, v = jnp.split(h @ w_kv, 2, axis=-1)
    n_blocks = -(-s // BLOCK_SIZE)
    pad = n_blocks * BLOCK_SIZE - s
    def to_blocks(t):
        t = t.reshape(b, s, N_HEADS, HEAD_DIM).transpose(0, 2, 1, 3)
        t = jnp.pad(t, ((0, 0), (0, 0), (0, pad), (0, 0)))
        return t.reshape(b, N_HEADS, n_blocks, BLOCK_SIZE, HEAD_DIM)
    k_blocks, v_blocks = to_blocks(k), to_blocks(v)
    k_mean = jnp.mean(k_blocks.astype(jnp.float32), axis=3)
    return k_blocks, v_blocks, k_mean

def moba_attention(q, k_blocks, v_blocks, k_mean):
    b, h, s, dh = q.shape
    n_blocks = k_blocks.shape[2]
    n_chunks = s // Q_CHUNK
    k_eff = min(TOP_K_BLOCKS, n_blocks)
    scale = dh ** -0.5
    slopes = alibi_slopes(h)[None, :, None, None]
    bi = jnp.arange(b)[:, None, None, None]
    hi = jnp.arange(h)[None, :, None, None]
    offs = jnp.arange(BLOCK_SIZE, dtype=jnp.int32)
    kbs = k_eff * BLOCK_SIZE

    def chunk(c):
        start = c * Q_CHUNK
        q_c = lax.dynamic_slice_in_dim(q, start, Q_CHUNK, axis=2)
        pos_q = start + jnp.arange(Q_CHUNK, dtype=jnp.int32)
        own = start // BLOCK_SIZE
        gate = jnp.einsum("bhqd,bhnd->bhqn", q_c.astype(jnp.float32), k_mean)
        gate = jnp.where(jnp.arange(n_blocks) < own, gate, -jnp.inf)
        _, idx = lax.top_k(gate, k_eff)
        sel_valid = idx < own
        k_sel = k_blocks[bi, hi, idx]
        v_sel = v_blocks[bi, hi, idx]
        s_sel = jnp.einsum("bhqd,bhqjsd->bhqjs", q_c, k_sel).astype(jnp.float32) * scale
        dist_sel = (pos_q[None, None, :, None, None] - (idx[..., None] * BLOCK_SIZE + offs)).astype(jnp.float32)
        s_sel = jnp.where(sel_valid[..., None], s_sel - slopes[..., None] * dist_sel, -jnp.inf)
        k_own = lax.dynamic_index_in_dim(k_blocks, own, axis=2, keepdims=False)
        v_own = lax.dynamic_index_in_dim(v_blocks, own, axis=2, keepdims=False)
        s_own = jnp.einsum("bhqd,bhsd->bhqs", q_c, k_own).astype(jnp.float32) * scale
        dist_own = pos_q[:, None] - (own * BLOCK_SIZE + offs)[None, :]
        s_own = jnp.where(dist_own >= 0, s_own - slopes * dist_own.astype(jnp.float32), -jnp.inf)
        logits = jnp.concatenate([s_sel.reshape(b, h, Q_CHUNK, kbs), s_own], axis=-1)
        p = jax.nn.softmax(logits, axis=-1)
        p_sel = p[..., :kbs].reshape(b, h, Q_CHUNK, k_eff, BLOCK_SIZE).astype(q.dtype)
        p_own = p[..., kbs:].astype(q.dtype)
        return (jnp.einsum("bhqjs,bhqjsd->bhqd", p_sel, v_sel)
                + jnp.einsum("bhqs,bhsd->bhqd", p_own, v_own))

    outs = lax.map(chunk, jnp.arange(n_chunks, dtype=jnp.int32))
    return outs.transpose(1, 2, 0, 3, 4).reshape(b, h, s, dh)

def setup_inputs(seed: int = 0) -> dict:
    key = jax.random.key(seed)
    ks = jax.random.split(key, 16)
    D, F = D_MODEL, D_FF
    def nrm(k, shape, fan_in):
        return jax.random.normal(k, shape, jnp.float32) * (fan_in ** -0.5)
    def gain(k, shape):
        return 1.0 + 0.05 * jax.random.normal(k, shape, jnp.float32)
    return {
        "x": jax.random.normal(ks[0], (BATCH, SEQ, D), jnp.float32),
        "norm_mix": gain(ks[1], (DEPTH, D)),
        "norm_ffn": gain(ks[2], (DEPTH, D)),
        "ffn_w_up": nrm(ks[3], (DEPTH, D, 2 * F), D),
        "ffn_conv": nrm(ks[4], (DEPTH, CONV_WIDTH, F), CONV_WIDTH),
        "ffn_conv_b": 0.01 * jax.random.normal(ks[5], (DEPTH, F), jnp.float32),
        "ffn_w_down": nrm(ks[6], (DEPTH, F, D), F),
        "a_w_in": nrm(ks[7], (N_A_LAYERS, D, 3 * D), D),
        "a_conv": nrm(ks[8], (N_A_LAYERS, CONV_WIDTH, D), CONV_WIDTH),
        "a_w_out": nrm(ks[9], (N_A_LAYERS, D, D), D),
        "kv_norm": gain(ks[10], (D,)),
        "w_kv": nrm(ks[11], (D, 2 * D), D),
        "b_w_q": nrm(ks[12], (N_B_LAYERS, D, D), D),
        "b_w_o": nrm(ks[13], (N_B_LAYERS, D, D), D),
        "final_norm": gain(ks[14], (D,)),
    }

def reference(x, norm_mix, norm_ffn, ffn_w_up, ffn_conv, ffn_conv_b, ffn_w_down,
              a_w_in, a_conv, a_w_out, kv_norm, w_kv, b_w_q, b_w_o, final_norm):
    b, s, d = x.shape
    k_blocks = v_blocks = k_mean = None
    for i in range(DEPTH):
        h = rmsnorm(x, norm_mix[i])
        if i < N_A_LAYERS:
            x = x + short_conv_mixer(h, a_w_in[i], a_conv[i], a_w_out[i])
        else:
            j = i - N_A_LAYERS
            q = (h @ b_w_q[j]).reshape(b, s, N_HEADS, HEAD_DIM).transpose(0, 2, 1, 3)
            o = moba_attention(q, k_blocks, v_blocks, k_mean)
            x = x + o.transpose(0, 2, 1, 3).reshape(b, s, d) @ b_w_o[j]
        x = x + conv_ffn(rmsnorm(x, norm_ffn[i]), ffn_w_up[i], ffn_conv[i], ffn_conv_b[i], ffn_w_down[i])
        if i == N_A_LAYERS - 1:
            k_blocks, v_blocks, k_mean = shared_kv(x, kv_norm, w_kv)
    return rmsnorm(x, final_norm)


_drawn_inputs = setup_inputs


def setup_inputs(seed=0):
    import zlib

    import numpy as np

    out = dict(_drawn_inputs(seed))
    spreads = {}
    factors = {'ffn_conv_b': 8.0, 'kv_norm': 3.929}
    for name, (base, spread) in spreads.items():
        noise = np.random.default_rng([zlib.crc32(name.encode()), seed]).standard_normal(out[name].shape)
        drawn = base * np.exp(spread * noise) if base else spread * noise
        out[name] = __import__('jax').numpy.asarray(drawn.astype(out[name].dtype))
    for name, factor in factors.items():
        out[name] = (out[name] * factor).astype(out[name].dtype)
    return out
```

```python
from contextlib import ExitStack

import concourse.bass as bass
from concourse import mybir

F32 = mybir.dt.float32
F32R = mybir.dt.float32r
ALU = mybir.AluOpType
ACT = mybir.ActivationFunctionType
AX_X = mybir.AxisListType.X

P = 128
EPS = 1e-6
RAW = 6
SPLIT = 3
MASKED = -1e30


def build(nc, x, norm_mix, norm_ffn, ffn_w_up, ffn_conv, ffn_conv_b, ffn_w_down,
          a_w_in, a_conv, a_w_out, kv_norm, w_kv, b_w_q, b_w_o, final_norm, out):
    _, S, D = x.shape
    F = ffn_conv.shape[2]
    KD = D // P
    NH = D // P
    TAPS = ffn_conv.shape[1]
    UNITS = F // (2 * P)
    FT = F // P
    COLS = KD * 256
    SCALE = float(P) ** -0.5
    SLOPE = [2.0 ** (-8.0 * (h + 1) / NH) for h in range(NH)]
    assert S == 2 * P and D == 1024 and UNITS * 2 * P == F and COLS == 2 * D and UNITS % 2 == 1

    A_IN, A_B, A_OUT = 0, KD, KD + KD // 2
    FFN = [A_OUT + KD // 2, 0]
    V0 = FFN[0] + 3 * UNITS
    KQ0 = V0 + KD // 2
    O0 = KQ0 + KD
    FFN[1] = O0 + KD // 2
    SLOTS = FFN[1] + 3 * UNITS

    TURN = 2 * 3
    assert TURN % RAW == 0 and TURN % SPLIT == 0
    TURNS = (UNITS - 3) // 2

    def gate_slot(l, j):
        return FFN[l] if j == 0 else FFN[l] + 3 * j - 1

    def after(n, turn, step):
        return n if turn is None else n + step * turn

    def rows(w):
        return w.rearrange("(k p) n -> p k n", p=P)

    in_rows, aout_rows = rows(a_w_in[0]), rows(a_w_out[0])
    kv_rows, q_rows, o_rows = rows(w_kv), rows(b_w_q[0]), rows(b_w_o[0])
    up_rows = [rows(ffn_w_up[l]) for l in range(2)]
    down_rows = [rows(ffn_w_down[l]) for l in range(2)]
    x_rows = x[0].rearrange("(t p) n -> p t n", p=P)
    out_rows = out[0].rearrange("(t p) n -> p t n", p=P)

    with ExitStack() as ctx:
        def sb(name, shape, dt=F32):
            return ctx.enter_context(nc.sbuf_tensor(name, shape, dt))

        def sem(name):
            return ctx.enter_context(nc.semaphore(name))

        raw = sb("raw", [P, RAW, COLS])
        w_hi = sb("w_hi", [P, SPLIT, COLS], F32R)
        w_lo = sb("w_lo", [P, SPLIT, COLS], F32R)
        xs = sb("xs", [P, 2, D])
        hA_hi = sb("hA_hi", [P, KD, S], F32R)
        hA_lo = sb("hA_lo", [P, KD, S], F32R)
        hB_hi = sb("hB_hi", [P, KD, S], F32R)
        hB_lo = sb("hB_lo", [P, KD, S], F32R)
        mix_hi = sb("mix_hi", [P, KD, S], F32R)
        mix_lo = sb("mix_lo", [P, KD, S], F32R)
        v_hi = sb("v_hi", [P, 2, D], F32R)
        v_lo = sb("v_lo", [P, 2, D], F32R)
        kq_hi = sb("kq_hi", [P, 2, 2, 512], F32R)
        kq_lo = sb("kq_lo", [P, 2, 2, 512], F32R)
        pt_hi = sb("pt_hi", [P, 2, 384], F32R)
        pt_lo = sb("pt_lo", [P, 2, 384], F32R)
        scratch = sb("scratch", [P, 2 * D])
        gain = sb("gain", [P, D])
        dist = sb("dist", [P, 384])
        ident = sb("ident", [P, P])
        par_rows = sb("par_rows", [P, 3, P])
        a_par = sb("a_par", [P, TAPS * KD])
        f_par = sb("f_par", [P, 2, (TAPS + 1) * FT])
        sumsq = sb("sumsq", [P, 2, 2])
        msq = sb("msq", [P, 2, 2])
        rstd = sb("rstd", [P, 2])
        minus_half = sb("minus_half", [P, 1])
        mx = sb("mx", [P, 2, 2])
        nbias = sb("nbias", [P, 2, 2])
        psums = sb("psums", [P, 2, 2])
        rinv = sb("rinv", [P, 2, 2])

        normed = scratch[:].rearrange("p (t n) -> p t n", t=2)
        conv_out = scratch[:].rearrange("p (f n) -> p f n", f=KD)
        glu = scratch[:, 0:1024].rearrange("p (b e n) -> p b e n", b=2, e=2)
        logits = scratch[:, 0:768].rearrange("p (e n) -> p e n", e=2)
        opening = scratch[:, 1024:2048].rearrange("p (b n) -> p b n", b=2)
        c_sb = gain[:, 0:512]
        cx = gain[:, 512:1024].rearrange("p (e n) -> p e n", e=2)
        act_hi = kq_hi[:].rearrange("p a b n -> p (a b n)")[:, 0:1024].rearrange("p (b e n) -> p b e n", b=2, e=2)
        act_lo = kq_lo[:].rearrange("p a b n -> p (a b n)")[:, 0:1024].rearrange("p (b e n) -> p b e n", b=2, e=2)

        bank = [ctx.enter_context(nc.psum_tensor(f"proj{i}", [P, 512], F32)) for i in range(2)]
        acc = [[ctx.enter_context(nc.psum_tensor(f"acc{t}{h}", [P, 512], F32)) for h in range(2)] for t in range(2)]
        tr = [ctx.enter_context(nc.psum_tensor(f"tr{i}", [P, 512], F32)) for i in range(2)]

        landed = [sem(f"landed{r}") for r in range(RAW)]
        x_in = [sem("x_in0"), sem("x_in1")]
        gain0_in = sem("gain0_in")
        gain_in = sem("gain_in")
        par_in = sem("par_in")
        consts = sem("consts")
        zeroed = sem("zeroed")
        w_hi_ready = sem("w_hi_ready")
        w_lo_ready = sem("w_lo_ready")
        slot_done = sem("slot_done")
        acc0_done = sem("acc0_done")
        par_T = sem("par_T")
        par_ready = sem("par_ready")
        x_new = sem("x_new")
        squared = sem("squared")
        ms_part = sem("ms_part")
        ms_full = sem("ms_full")
        rstd_ready = sem("rstd_ready")
        normed_ready = sem("normed_ready")
        x_T = sem("x_T")
        opening_copied = sem("opening_copied")
        opening_T = sem("opening_T")
        first_landed = sem("first_landed")
        first_hi = sem("first_hi")
        first_lo = sem("first_lo")
        h_hi_ready = sem("h_hi_ready")
        h_lo_ready = sem("h_lo_ready")
        c_copied = sem("c_copied")
        cx_ready = sem("cx_ready")
        a_conv_op = sem("a_conv_op")
        a_conv_done = sem("a_conv_done")
        gated = sem("gated")
        mix_hi_ready = sem("mix_hi_ready")
        mix_lo_ready = sem("mix_lo_ready")
        tap0 = sem("tap0")
        conv_op = sem("conv_op")
        silu_done = sem("silu_done")
        act_full = sem("act_full")
        act_hi_ready = sem("act_hi_ready")
        act_lo_ready = sem("act_lo_ready")
        v_hi_ready = sem("v_hi_ready")
        v_lo_ready = sem("v_lo_ready")
        kq_hi_ready = sem("kq_hi_ready")
        kq_lo_ready = sem("kq_lo_ready")
        scores_ready = sem("scores_ready")
        logits_ready = sem("logits_ready")
        max_ready = sem("max_ready")
        nbias_ready = sem("nbias_ready")
        exp_ready = sem("exp_ready")
        rinv_ready = sem("rinv_ready")
        probs_ready = sem("probs_ready")
        probs_T = sem("probs_T")
        pt_hi_ready = sem("pt_hi_ready")
        pt_lo_ready = sem("pt_lo_ready")
        heads_out = sem("heads_out")
        stored = sem("stored")

        STAT = [0, 1, 2, 2, 3, 4]
        GAIN = [norm_mix[0], norm_ffn[0], kv_norm, norm_mix[1], norm_ffn[1], final_norm]
        HID = [(hA_hi, hA_lo), (hA_hi, hA_lo), (hA_hi, hA_lo), (hB_hi, hB_lo), (hA_hi, hA_lo)]
        LAST = [A_OUT + KD // 2 - 1, FFN[0] + 3 * UNITS - 1, O0 + KD // 2 - 1, FFN[1] + 3 * UNITS - 1]

        def step4(n, t, h):
            return 4 * n + 2 * t + h + 1

        block = ctx.enter_context(nc.Block())

        @block.sync
        def _(sp):
            def load(s, src, turn=None):
                if s >= RAW:
                    sp.wait_ge(w_lo_ready, after(s - RAW + 1, turn, TURN))
                sp.dma_start(raw[:, s % RAW, :].rearrange("p (k n) -> p k n", k=src.shape[1]), src).then_inc(landed[s % RAW], 16)

            def wide(w, c0):
                return w[:, :, bass.ds(c0, 256)]

            def ffn_loads(l, j, turn=None):
                s, at = gate_slot(l, j), after(j, turn, 2)
                load(s, wide(up_rows[l], at * 256), turn)
                load(s + 1, wide(up_rows[l], at * 256 + F), turn)
                if j:
                    load(s + 2, down_rows[l][:, bass.ds(at * 2 - 2, 2), :], turn)

            def ffn_stream(l):
                ffn_loads(l, 0)
                with sp.Fori(0, TURNS) as turn:
                    ffn_loads(l, 1, turn)
                    ffn_loads(l, 2, turn)
                for j in (UNITS - 2, UNITS - 1):
                    ffn_loads(l, j)
                load(FFN[l] + 3 * UNITS - 1, down_rows[l][:, 2 * UNITS - 2:2 * UNITS, :])

            sp.dma_start(xs[:, 0, :], x_rows[:, 0, :]).then_inc(x_in[0], 16)
            sp.dma_start(gain[:], GAIN[0].rearrange("(a n) -> a n", a=1).to_broadcast([P, D])).then_inc(gain0_in, 16)
            sp.dma_start(xs[:, 1, :], x_rows[:, 1, :]).then_inc(x_in[1], 16)
            halves = raw[:, 0, :].rearrange("p (g k n) -> p g k n", g=2, n=256)
            for g, landing in enumerate((first_landed, landed[0])):
                sp.dma_start(halves[:, g], in_rows[:, 4 * g:4 * g + 4, D:D + 256]).then_inc(landing, 16)
            load(1, wide(in_rows, 2 * D))
            load(2, wide(in_rows, D + 256))
            sp.dma_start(par_rows[0:TAPS * KD, 0, :], a_conv[0].rearrange("t (k n) -> (t k) n", n=P)).then_inc(par_in, 16)
            for l in range(2):
                sp.dma_start(par_rows[0:TAPS * FT, 1 + l, :],
                             ffn_conv[l].rearrange("t (k n) -> (t k) n", n=P)).then_inc(par_in, 16)
                sp.dma_start(par_rows[TAPS * FT:(TAPS + 1) * FT, 1 + l, :],
                             ffn_conv_b[l].rearrange("(k n) -> k n", n=P)).then_inc(par_in, 16)
            load(3, wide(in_rows, 2 * D + 256))
            for i in range(2, KD // 2):
                load(A_IN + 2 * i, wide(in_rows, D + 256 * i))
                load(A_IN + 2 * i + 1, wide(in_rows, 2 * D + 256 * i))
            for i in range(KD // 2):
                load(A_B + i, wide(in_rows, 256 * i))
            for i in range(KD // 2):
                load(A_OUT + i, aout_rows[:, 2 * i:2 * i + 2, :])
            ffn_stream(0)
            for i in range(KD // 2):
                load(V0 + i, wide(kv_rows, D + 256 * i))
            for i in range(KD // 2):
                load(KQ0 + 2 * i, wide(kv_rows, 256 * i))
                load(KQ0 + 2 * i + 1, wide(q_rows, 256 * i))
            for i in range(KD // 2):
                load(O0 + i, o_rows[:, 2 * i:2 * i + 2, :])
            ffn_stream(1)
            for t in range(2):
                for h in range(2):
                    sp.wait_ge(normed_ready, step4(5, t, h))
                    sp.dma_start(out_rows[:, t, 512 * h:512 * h + 512],
                                 normed[:, t, 512 * h:512 * h + 512]).then_inc(stored, 16)
            sp.wait_ge(stored, 64)

        @block.gpsimd
        def _(pool):
            def load_gain(n):
                pool.dma_start(gain[:], GAIN[n].rearrange("(a n) -> a n", a=1).to_broadcast([P, D])).then_inc(gain_in, 16)

            def root(z, t):
                pool.wait_ge(ms_full, 2 * z + t + 1)
                pool.tensor_tensor(rstd[:, t:t + 1], msq[:, t, 1:2], minus_half[:], ALU.pow).then_inc(rstd_ready, 1)

            pool.memset(ident[:], 0.0).then_inc(zeroed, 1)
            pool.memset(minus_half[:], -0.5).then_inc(zeroed, 1)
            pool.wait_ge(zeroed, 2)
            pool.affine_select(out=ident[:], in_=ident[:], compare_op=ALU.not_equal, fill=1.0, base=0,
                               pattern=[[-1, P]], channel_multiplier=1).then_inc(consts, 1)
            pool.iota(dist[:, 0:128], pattern=[[1, 128]], base=0, channel_multiplier=-1,
                      allow_small_or_imprecise_dtypes=True).then_inc(zeroed, 1)
            pool.iota(dist[:, 128:384], pattern=[[1, 256]], base=-P, channel_multiplier=-1,
                      allow_small_or_imprecise_dtypes=True).then_inc(zeroed, 1)
            pool.wait_ge(zeroed, 4)
            pool.affine_select(out=dist[:, 0:128], in_=dist[:, 0:128], compare_op=ALU.is_ge, fill=MASKED, base=0,
                               pattern=[[-1, 128]], channel_multiplier=1).then_inc(consts, 1)
            pool.affine_select(out=dist[:, 128:384], in_=dist[:, 128:384], compare_op=ALU.is_ge, fill=MASKED, base=P,
                               pattern=[[-1, 256]], channel_multiplier=1).then_inc(consts, 1)
            root(0, 0)
            root(0, 1)
            pool.wait_ge(a_conv_done, KD)
            load_gain(1)
            root(1, 0)
            root(1, 1)
            pool.wait_ge(normed_ready, step4(1, 1, 1))
            load_gain(2)
            root(2, 0)
            root(2, 1)
            pool.wait_ge(normed_ready, step4(2, 1, 1))
            load_gain(3)
            pool.wait_ge(normed_ready, step4(3, 1, 1))
            load_gain(4)
            root(3, 0)
            root(3, 1)
            pool.wait_ge(normed_ready, step4(4, 1, 1))
            load_gain(5)
            root(4, 0)
            root(4, 1)

        @block.scalar
        def _(act):
            def hi(s, turn=None):
                if s >= SLOTS:
                    return
                act.wait_ge(landed[s % RAW], after(16 * (s // RAW + 1), turn, 16))
                if s >= SPLIT:
                    act.wait_ge(slot_done, after(s - SPLIT + 1, turn, TURN))
                act.activation(w_hi[:, s % SPLIT, :], raw[:, s % RAW, :], ACT.Copy).then_inc(w_hi_ready, 1)

            def square(z, t, h):
                part = xs[:, t, 512 * h:512 * h + 512]
                if z == 0:
                    act.wait_ge(x_in[t], 16)
                else:
                    act.wait_ge(x_new, step4(z - 1, t, h))
                act.activation(normed[:, t, 512 * h:512 * h + 512], part, ACT.Square,
                               accum_out=sumsq[:, t, h:h + 1]).then_inc(squared, 1)

            def h_hi(n, t, h):
                act.wait_ge(x_T, step4(n, t, h))
                act.activation(HID[n][0][:, 4 * h:4 * h + 4, P * t:P * t + P],
                               tr[h][:].rearrange("p (k n) -> p k n", k=4), ACT.Copy).then_inc(h_hi_ready, 1)

            def boundary(r, n):
                for h in range(2):
                    square(r + 1, 0, h)
                if n < 5:
                    hi(LAST[r] + 2)
                    for h in range(2):
                        h_hi(n, 0, h)
                for h in range(2):
                    square(r + 1, 1, h)
                if n < 5:
                    for h in range(2):
                        h_hi(n, 1, h)

            def copy_opening(s, b, o):
                act.wait_ge(slot_done, s + b + 1)
                act.activation(opening[:, b, :], bank[b][:], ACT.Copy).then_inc(opening_copied, 1)

            def unit(l, j, turn=None):
                s, U = gate_slot(l, j), l * UNITS + j
                g = glu[:, U % 2]
                gate = bank[0] if j else tr[0]
                if j:
                    act.wait_ge(slot_done, after(s + 1, turn, TURN))
                else:
                    hi(s + 2)
                    copy_opening(s, 0, l + 1)
                    hi(s + 3)
                    copy_opening(s, 1, l + 1)
                    act.wait_ge(opening_T, 2 * (l + 1) + 1)
                for e in range(2):
                    f = after(2 * j + e, turn, 4)
                    ins = act.activation(g[:, e, :], gate[:, 256 * e:256 * e + 256], ACT.Identity,
                                         bias=f_par[:, l, bass.ds(f + TAPS * FT, 1)],
                                         scale=f_par[:, l, bass.ds(f + (TAPS - 1) * FT, 1)])
                ins.then_inc(tap0, 1)
                hi(s + 3 if j else s + 4, turn)
                act.wait_ge(conv_op, after(4 * U + 4, turn, 8))
                act.activation(g, g, ACT.Silu).then_inc(silu_done, 1)
                act.wait_ge(act_full, after(U + 1, turn, 2))
                act.activation(act_hi[:, U % 2], g, ACT.Copy).then_inc(act_hi_ready, 1)
                if j:
                    hi(s + 4, turn)
                    if j < UNITS - 1:
                        hi(s + 5, turn)

            def ffn(l):
                unit(l, 0)
                with act.Fori(0, TURNS) as turn:
                    unit(l, 1, turn)
                    unit(l, 2, turn)
                unit(l, UNITS - 2)
                unit(l, UNITS - 1)

            def exp(h):
                e = h % 2
                act.wait_ge(nbias_ready, h + 1)
                for t, cols in ((0, slice(0, 128)), (1, slice(128, 384))):
                    act.activation(logits[:, e, cols], logits[:, e, cols], ACT.Exp, bias=nbias[:, e, t:t + 1],
                                   scale=SCALE, accum_out=psums[:, e, t:t + 1]).then_inc(exp_ready, 1)

            def kq(i):
                act.wait_ge(slot_done, KQ0 + i + 1)
                act.activation(kq_hi[:, i // 2 % 2, i % 2, :], bank[i % 2][:], ACT.Copy).then_inc(kq_hi_ready, 1)

            def v(i):
                act.wait_ge(slot_done, V0 + i + 1)
                act.activation(v_hi[:, :, 256 * i:256 * i + 256],
                               bank[i % 2][:].rearrange("p (t n) -> p t n", t=2), ACT.Copy).then_inc(v_hi_ready, 1)

            def first_half_hi():
                act.wait_ge(first_landed, 16)
                act.activation(w_hi[:, 0, 0:COLS // 2], raw[:, 0, 0:COLS // 2], ACT.Copy).then_inc(first_hi, 1)

            for h in range(2):
                square(0, 0, h)
            for h in range(2):
                h_hi(0, 0, h)
            for h in range(2):
                square(0, 1, h)
            first_half_hi()
            act.wait_ge(landed[0], 16)
            act.activation(w_hi[:, 0, COLS // 2:], raw[:, 0, COLS // 2:], ACT.Copy).then_inc(w_hi_ready, 1)
            for h in range(2):
                h_hi(0, 1, h)
            hi(1)
            hi(2)
            for i in range(KD // 2):
                if i == 0:
                    for b in range(2):
                        copy_opening(A_IN, b, 0)
                        hi(3 + b)
                    act.wait_ge(opening_T, 1)
                else:
                    act.wait_ge(slot_done, A_IN + 2 * i + 1)
                    act.wait_ge(cx_ready, i)
                act.activation(c_sb, (bank[0] if i else tr[0])[:], ACT.Copy).then_inc(c_copied, 1)
                if i:
                    hi(2 * i + 3)
                    hi(2 * i + 4)

            def mixed(i):
                act.wait_ge(gated, i + 1)
                act.activation(mix_hi[:, 2 * i:2 * i + 2, :], conv_out[:, 2 * i:2 * i + 2, :],
                               ACT.Copy).then_inc(mix_hi_ready, 1)

            for i in range(KD // 2 - 1):
                mixed(i)
                hi(A_B + i + 3)
            mixed(KD // 2 - 1)
            hi(A_OUT + 2)
            hi(A_OUT + 3)
            hi(A_OUT + 4)
            boundary(0, 1)
            ffn(0)
            boundary(1, 2)

            hi(V0 + 2)
            for i in range(KD // 2):
                v(i)
                if i >= 2:
                    for h in range(2):
                        h_hi(3, i - 2, h)
                hi(V0 + i + 3)
            kq(0)
            hi(KQ0 + 3)
            for p in range(NH // 2):
                kq(2 * p + 1)
                hi(KQ0 + 2 * p + 4)
                exp(2 * p)
                exp(2 * p + 1)
                if p < NH // 2 - 1:
                    kq(2 * p + 2)
                for e in range(2):
                    act.wait_ge(probs_T, 2 * p + e + 1)
                    act.activation(pt_hi[:, e, :], tr[e][:, 0:384], ACT.Copy).then_inc(pt_hi_ready, 1)
                hi(KQ0 + 2 * p + 5)
                for e in range(2):
                    act.wait_ge(heads_out, 2 * p + e + 1)
                    act.activation(mix_hi[:, 2 * p + e, :], tr[e][:, 0:256], ACT.Copy).then_inc(mix_hi_ready, 1)
            hi(O0 + 4)
            boundary(2, 4)
            ffn(1)
            boundary(3, 5)

        @block.vector
        def _(dve):
            def lo(s, turn=None):
                if s >= SLOTS:
                    return
                dve.wait_ge(w_hi_ready, after(s + 1, turn, TURN))
                dve.tensor_tensor(w_lo[:, s % SPLIT, :], raw[:, s % RAW, :], w_hi[:, s % SPLIT, :].bitcast(F32),
                                  ALU.subtract).then_inc(w_lo_ready, 1)

            def residual(r, t):
                if t == 0:
                    dve.wait_ge(acc0_done, r + 1)
                else:
                    dve.wait_ge(slot_done, LAST[r] + 1)
                for h in range(2):
                    part = xs[:, t, 512 * h:512 * h + 512]
                    dve.tensor_tensor(part, part, acc[t][h][:], ALU.add).then_inc(x_new, 1)

            def mean_square(z, t):
                dve.wait_ge(squared, step4(z, t, 0))
                dve.tensor_scalar(msq[:, t, 0:1], sumsq[:, t, 0:1], 1.0 / D, EPS, ALU.mult, ALU.add).then_inc(ms_part, 1)
                dve.wait_ge(squared, step4(z, t, 1))
                dve.wait_ge(ms_part, 2 * z + t + 1)
                dve.tensor_scalar(msq[:, t, 1:2], sumsq[:, t, 1:2], 1.0 / D, msq[:, t, 0:1],
                                  ALU.mult, ALU.add).then_inc(ms_full, 1)

            def normalise(n, t):
                dve.wait_ge(*((gain_in, 16 * n) if n else (gain0_in, 16)))
                dve.wait_ge(rstd_ready, 2 * STAT[n] + t + 1)
                for h in range(2):
                    cols = slice(512 * h, 512 * h + 512)
                    dve.scalar_tensor_tensor(out=normed[:, t, cols], in0=xs[:, t, cols], scalar=rstd[:, t:t + 1],
                                             in1=gain[:, cols], op0=ALU.mult, op1=ALU.mult).then_inc(normed_ready, 1)

            def h_lo(n, t):
                for h in range(2):
                    dve.wait_ge(h_hi_ready, step4(n, t, h))
                    dve.tensor_tensor(HID[n][1][:, 4 * h:4 * h + 4, P * t:P * t + P],
                                      tr[h][:].rearrange("p (k n) -> p k n", k=4),
                                      HID[n][0][:, 4 * h:4 * h + 4, P * t:P * t + P].bitcast(F32),
                                      ALU.subtract).then_inc(h_lo_ready, 1)

            def boundary(r, n):
                residual(r, 0)
                mean_square(r + 1, 0)
                normalise(n, 0)
                if n < 5:
                    lo(LAST[r] + 2)
                    h_lo(n, 0)
                residual(r, 1)
                mean_square(r + 1, 1)
                normalise(n, 1)
                if n < 5:
                    h_lo(n, 1)

            def unit(l, j, turn=None):
                s, U = gate_slot(l, j), l * UNITS + j
                g = glu[:, U % 2]
                gate, up = bank if j else tr
                if j == 0:
                    lo(s + 2)
                    lo(s + 3)
                dve.wait_ge(tap0, after(U + 1, turn, 2))
                for back in (1, 2):
                    for e in range(2):
                        if back == 2:
                            dve.wait_ge(conv_op, after(4 * U + e + 1, turn, 8))
                        f = after(2 * j + e, turn, 4)
                        dst = g[:, e, back:S]
                        dve.scalar_tensor_tensor(out=dst, in0=gate[:, 256 * e:256 * e + S - back],
                                                 scalar=f_par[:, l, bass.ds(f + (TAPS - 1 - back) * FT, 1)],
                                                 in1=dst, op0=ALU.mult, op1=ALU.add).then_inc(conv_op, 1)
                lo(s + 3 if j else s + 4, turn)
                if j:
                    dve.wait_ge(slot_done, after(s + 2, turn, TURN))
                else:
                    dve.wait_ge(opening_T, 2 * (l + 1) + 2)
                dve.wait_ge(silu_done, after(U + 1, turn, 2))
                dve.tensor_tensor(g, g, up[:].rearrange("p (e n) -> p e n", e=2), ALU.mult).then_inc(act_full, 1)
                dve.wait_ge(act_hi_ready, after(U + 1, turn, 2))
                dve.tensor_tensor(act_lo[:, U % 2], g, act_hi[:, U % 2].bitcast(F32),
                                  ALU.subtract).then_inc(act_lo_ready, 1)
                if j:
                    lo(s + 4, turn)
                    if j < UNITS - 1:
                        lo(s + 5, turn)

            def ffn(l):
                unit(l, 0)
                with dve.Fori(0, TURNS) as turn:
                    unit(l, 1, turn)
                    unit(l, 2, turn)
                unit(l, UNITS - 2)
                unit(l, UNITS - 1)

            def conv_a(i):
                if i:
                    dve.wait_ge(slot_done, A_IN + 2 * i + 2)
                else:
                    dve.wait_ge(opening_T, 2)
                dve.wait_ge(c_copied, i + 1)
                if i:
                    dve.wait_ge(a_conv_done, 2 * i)
                dve.tensor_tensor(cx, c_sb.rearrange("p (e n) -> p e n", e=2),
                                  (bank[1] if i else tr[1])[:].rearrange("p (e n) -> p e n", e=2),
                                  ALU.mult).then_inc(cx_ready, 1)
                dve.wait_ge(cx_ready, i + 1)
                for e in range(2):
                    f = 2 * i + e
                    tap = [a_par[:, c * KD + f:c * KD + f + 1] for c in range(TAPS)]
                    dve.tensor_scalar(conv_out[:, f, :], cx[:, e, :], tap[2], None, ALU.mult).then_inc(a_conv_op, 1)
                    dve.wait_ge(a_conv_op, 2 * f + 1)
                    dve.scalar_tensor_tensor(out=conv_out[:, f, 1:S], in0=cx[:, e, 0:S - 1], scalar=tap[1],
                                             in1=conv_out[:, f, 1:S], op0=ALU.mult, op1=ALU.add).then_inc(a_conv_op, 1)
                    dve.wait_ge(a_conv_op, 2 * f + 2)
                    dve.scalar_tensor_tensor(out=conv_out[:, f, 2:S], in0=cx[:, e, 0:S - 2], scalar=tap[0],
                                             in1=conv_out[:, f, 2:S], op0=ALU.mult, op1=ALU.add).then_inc(a_conv_done, 1)

            def gate_a(i):
                dve.wait_ge(slot_done, A_B + i + 1)
                dve.wait_ge(a_conv_done, 2 * i + 2)
                dst = conv_out[:, 2 * i:2 * i + 2, :]
                dve.tensor_tensor(dst, dst, bank[i % 2][:].rearrange("p (e n) -> p e n", e=2), ALU.mult).then_inc(gated, 1)
                dve.wait_ge(mix_hi_ready, i + 1)
                dve.tensor_tensor(mix_lo[:, 2 * i:2 * i + 2, :], dst, mix_hi[:, 2 * i:2 * i + 2, :].bitcast(F32),
                                  ALU.subtract).then_inc(mix_lo_ready, 1)

            def kq(i):
                dve.wait_ge(kq_hi_ready, i + 1)
                dve.tensor_tensor(kq_lo[:, i // 2 % 2, i % 2, :], bank[i % 2][:],
                                  kq_hi[:, i // 2 % 2, i % 2, :].bitcast(F32), ALU.subtract).then_inc(kq_lo_ready, 1)

            def v(i):
                dve.wait_ge(v_hi_ready, i + 1)
                cols = slice(256 * i, 256 * i + 256)
                dve.tensor_tensor(v_lo[:, :, cols], bank[i % 2][:].rearrange("p (t n) -> p t n", t=2),
                                  v_hi[:, :, cols].bitcast(F32), ALU.subtract).then_inc(v_lo_ready, 1)

            def row_max(h):
                e = h % 2
                dve.wait_ge(scores_ready, h + 1)
                dve.scalar_tensor_tensor(out=logits[:, e, :], in0=dist[:], scalar=SLOPE[h] / SCALE, in1=tr[e][:, 0:384],
                                         op0=ALU.mult, op1=ALU.add).then_inc(logits_ready, 1)
                dve.wait_ge(logits_ready, h + 1)
                dve.reduce_max(mx[:, e, 0:1], logits[:, e, 0:128], AX_X).then_inc(max_ready, 1)
                dve.reduce_max(mx[:, e, 1:2], logits[:, e, 128:384], AX_X).then_inc(max_ready, 1)
                dve.wait_ge(max_ready, 2 * h + 2)
                dve.tensor_scalar(nbias[:, e, :], mx[:, e, :], -SCALE, None, ALU.mult).then_inc(nbias_ready, 1)

            def normal_probs(h):
                e = h % 2
                dve.wait_ge(exp_ready, 2 * h + 2)
                dve.reciprocal(rinv[:, e, :], psums[:, e, :]).then_inc(rinv_ready, 1)
                dve.wait_ge(rinv_ready, h + 1)
                for t, cols in ((0, slice(0, 128)), (1, slice(128, 384))):
                    dve.tensor_scalar(logits[:, e, cols], logits[:, e, cols], rinv[:, e, t:t + 1], None,
                                      ALU.mult).then_inc(probs_ready, 1)

            mean_square(0, 0)
            normalise(0, 0)
            h_lo(0, 0)
            mean_square(0, 1)
            normalise(0, 1)
            dve.wait_ge(first_hi, 1)
            dve.tensor_tensor(w_lo[:, 0, 0:COLS // 2], raw[:, 0, 0:COLS // 2], w_hi[:, 0, 0:COLS // 2].bitcast(F32),
                              ALU.subtract).then_inc(first_lo, 1)
            dve.wait_ge(w_hi_ready, 1)
            dve.tensor_tensor(w_lo[:, 0, COLS // 2:], raw[:, 0, COLS // 2:], w_hi[:, 0, COLS // 2:].bitcast(F32),
                              ALU.subtract).then_inc(w_lo_ready, 1)
            h_lo(0, 1)
            lo(1)
            lo(2)
            dve.wait_ge(par_T, 1)
            dve.tensor_copy(a_par[:], acc[0][0][:, 0:TAPS * KD]).then_inc(par_ready, 1)
            for l in range(2):
                dve.tensor_copy(f_par[:, l, :], acc[1][l][:, 0:(TAPS + 1) * FT]).then_inc(par_ready, 1)
            dve.wait_ge(par_ready, 3)
            lo(3)
            lo(4)
            for i in range(KD // 2):
                if i:
                    lo(2 * i + 3)
                conv_a(i)
                if i:
                    lo(2 * i + 4)
            for i in range(KD // 2 - 1):
                gate_a(i)
                lo(A_B + i + 3)
            gate_a(KD // 2 - 1)
            lo(A_OUT + 2)
            lo(A_OUT + 3)
            lo(A_OUT + 4)
            boundary(0, 1)
            ffn(0)
            boundary(1, 2)

            dve.wait_ge(consts, 3)
            lo(V0 + 2)
            for i in range(KD // 2):
                v(i)
                if i < 2:
                    normalise(3, i)
                else:
                    h_lo(3, i - 2)
                lo(V0 + i + 3)
            kq(0)
            lo(KQ0 + 3)
            for p in range(NH // 2):
                kq(2 * p + 1)
                lo(KQ0 + 2 * p + 4)
                for e in range(2):
                    row_max(2 * p + e)
                for e in range(2):
                    normal_probs(2 * p + e)
                if p < NH // 2 - 1:
                    kq(2 * p + 2)
                for e in range(2):
                    dve.wait_ge(pt_hi_ready, 2 * p + e + 1)
                    dve.tensor_tensor(pt_lo[:, e, :], tr[e][:, 0:384], pt_hi[:, e, :].bitcast(F32),
                                      ALU.subtract).then_inc(pt_lo_ready, 1)
                lo(KQ0 + 2 * p + 5)
                for e in range(2):
                    dve.wait_ge(mix_hi_ready, KD // 2 + 2 * p + e + 1)
                    dve.tensor_tensor(mix_lo[:, 2 * p + e, :], tr[e][:, 0:256], mix_hi[:, 2 * p + e, :].bitcast(F32),
                                      ALU.subtract).then_inc(mix_lo_ready, 1)
            lo(O0 + 4)
            boundary(2, 4)
            ffn(1)
            boundary(3, 5)

        @block.tensor
        def _(pe):
            def split_matmul(dst, parts, first, last):
                (sh, sl), (mh, ml) = parts
                pe.matmul(dst, sh, mh, start=first, stop=False)
                pe.matmul(dst, sh, ml, start=False, stop=False)
                return pe.matmul(dst, sl, mh, start=False, stop=last)

            def wait_slot(s, turn=None):
                pe.wait_ge(w_lo_ready, after(s + 1, turn, TURN))

            def project(s, b, hid, e):
                ring = s % SPLIT
                for k in range(KD):
                    w = slice(256 * k + P * e, 256 * k + P * e + P)
                    last = split_matmul(bank[b][:, 256 * e:256 * e + S],
                                        ((w_hi[:, ring, w], w_lo[:, ring, w]), (hid[0][:, k, :], hid[1][:, k, :])),
                                        k == 0, k == KD - 1)
                return last

            def project_rows(s, b, t, n=None):
                tok = slice(P * t, P * t + P)
                ring = s % SPLIT
                for k in range(KD):
                    if n is not None and k % 4 == 0:
                        pe.wait_ge(h_lo_ready, step4(n, t, k // 4))
                    if s == 0 and k % 4 == 0 and t == 0:
                        pe.wait_ge(*((w_lo_ready, 1) if k else (first_lo, 1)))
                    w = slice(256 * k, 256 * k + 256)
                    last = split_matmul(bank[b][:, 256 * t:256 * t + 256],
                                        ((hA_hi[:, k, tok], hA_lo[:, k, tok]), (w_hi[:, ring, w], w_lo[:, ring, w])),
                                        k == 0, k == KD - 1)
                return last

            def accumulate(s, left, t, e, first=False, final=False):
                ah, al = [part[:, P * t:P * t + P] for part in left[e]]
                wh, wl = [[w[:, s % SPLIT, D * e + 512 * h:D * e + 512 * h + 512] for h in range(2)] for w in (w_hi, w_lo)]
                for h in range(2):
                    pe.matmul(acc[t][h][:], ah, wh[h], start=first, stop=False)
                for h in range(2):
                    pe.matmul(acc[t][h][:], ah, wl[h], start=False, stop=False)
                for h in range(2):
                    last = pe.matmul(acc[t][h][:], al, wh[h], start=False, stop=final)
                return last

            def transposes(n, t):
                for h in range(2):
                    pe.wait_ge(normed_ready, step4(n, t, h))
                    if n or t:
                        pe.wait_ge(h_lo_ready, step4(n, t, h) - 2)
                    for k in range(4):
                        last = pe.transpose(tr[h][:, P * k:P * k + P],
                                            normed[:, t, 512 * h + P * k:512 * h + P * k + P], ident[:])
                    last.then_inc(x_T, 1)

            def finish(sA, leftA, ready_A, leftB, ready_B, n):
                sB = sA + 1
                wait_slot(sA)
                pe.wait_ge(*ready_A)
                for e in range(2):
                    accumulate(sA, leftA, 0, e)
                wait_slot(sB)
                pe.wait_ge(*ready_B)
                for e in range(2):
                    last = accumulate(sB, leftB, 0, e, final=(e == 1))
                last.then_inc(acc0_done, 1)
                for e in range(2):
                    last = accumulate(sA, leftA, 1, e)
                last.then_inc(slot_done, 1)
                accumulate(sB, leftB, 1, 0)
                if n < 5:
                    transposes(n, 0)
                accumulate(sB, leftB, 1, 1, final=True).then_inc(slot_done, 1)

            def open_rows(s, n):
                for t in range(2):
                    if t == 1:
                        transposes(n, 1)
                    for b in range(2):
                        if t == 0:
                            wait_slot(s + b)
                        last = project_rows(s + b, b, t, n)
                        if t == 1:
                            last.then_inc(slot_done, 1)

            def turn_opening(o):
                for b in range(2):
                    pe.wait_ge(opening_copied, 2 * o + b + 1)
                    for e in range(2):
                        for t in range(2):
                            last = pe.transpose(tr[b][:, 256 * e + P * t:256 * e + P * t + P],
                                                opening[:, b, 256 * t + P * e:256 * t + P * e + P], ident[:])
                    last.then_inc(opening_T, 1)

            def wide_after_opening(s, b, o):
                pe.wait_ge(opening_copied, 2 * o + b + 1)
                wait_slot(s)
                project(s, b, hidA, 0)
                if b == 0:
                    turn_opening(o)
                project(s, b, hidA, 1).then_inc(slot_done, 1)

            def wide_slot(s, b, hid, turn=None):
                wait_slot(s, turn)
                for e in range(2):
                    last = project(s, b, hid, e)
                last.then_inc(slot_done, 1)

            def deep_slot(s, left, first=False, turn=None):
                wait_slot(s, turn)
                for t in range(2):
                    for e in range(2):
                        last = accumulate(s, left, t, e, first=(first and e == 0))
                last.then_inc(slot_done, 1)

            def mix_pair(i):
                return [(mix_hi[:, 2 * i + e, :], mix_lo[:, 2 * i + e, :]) for e in range(2)]

            def act_pair(U):
                return [(act_hi[:, U % 2, e, :], act_lo[:, U % 2, e, :]) for e in range(2)]

            hidA, hidB = HID[0], HID[3]

            def gate_up(l, j, turn=None):
                s, U = gate_slot(l, j), l * UNITS + j
                pe.wait_ge(conv_op, after(4 * U, turn, 8))
                wide_slot(s, 0, hidA, turn)
                pe.wait_ge(act_full, after(U, turn, 2))
                wide_slot(s + 1, 1, hidA, turn)

            def down(l, j, turn=None):
                U = l * UNITS + j - 1
                pe.wait_ge(act_lo_ready, after(U + 1, turn, 2))
                deep_slot(gate_slot(l, j) + 2, act_pair(U), first=(j == 1), turn=turn)

            def ffn(l, n, next_n):
                open_rows(FFN[l], n)
                for b in range(2):
                    wide_after_opening(gate_slot(l, 1) + b, b, l + 1)
                pe.wait_ge(x_new, 4 * (2 * l + 1))
                down(l, 1)
                with pe.Fori(0, TURNS) as turn:
                    for j in (2, 3):
                        gate_up(l, j, turn)
                        down(l, j, turn)
                j = UNITS - 1
                U = l * UNITS + j
                gate_up(l, j)
                finish(gate_slot(l, j) + 2, act_pair(U - 1), (act_lo_ready, U), act_pair(U), (act_lo_ready, U + 1), next_n)

            pe.wait_ge(consts, 1)
            transposes(0, 0)
            project_rows(0, 0, 0, 0)
            transposes(0, 1)
            project_rows(0, 0, 1, 0).then_inc(slot_done, 1)
            wait_slot(1)
            project_rows(1, 1, 0)
            project_rows(1, 1, 1).then_inc(slot_done, 1)
            pe.wait_ge(par_in, 16 * 5)
            R0, R1 = TAPS * KD, (TAPS + 1) * FT
            pe.transpose(acc[0][0][:, 0:R0], par_rows[0:R0, 0, :], ident[0:R0, 0:R0])
            for l in range(2):
                last = pe.transpose(acc[1][l][:, 0:R1], par_rows[0:R1, 1 + l, :], ident[0:R1, 0:R1])
            last.then_inc(par_T, 1)
            for b in range(2):
                wide_after_opening(A_IN + 2 + b, b, 0)
            for i in range(2, KD // 2):
                pe.wait_ge(c_copied, i)
                wide_slot(A_IN + 2 * i, 0, hidA)
                pe.wait_ge(cx_ready, i)
                wide_slot(A_IN + 2 * i + 1, 1, hidA)
            for i in range(KD // 2):
                pe.wait_ge(*[(c_copied, KD // 2), (cx_ready, KD // 2)][i] if i < 2 else (gated, i - 1))
                wide_slot(A_B + i, i % 2, hidA)
            pe.wait_ge(par_ready, 3)
            for i in range(KD // 2 - 2):
                pe.wait_ge(mix_lo_ready, i + 1)
                deep_slot(A_OUT + i, mix_pair(i), first=(i == 0))
            i = KD // 2 - 2
            finish(A_OUT + i, mix_pair(i), (mix_lo_ready, i + 1), mix_pair(i + 1), (mix_lo_ready, i + 2), 1)

            ffn(0, 1, 2)

            open_rows(V0, 2)
            for i in range(2, KD // 2):
                pe.wait_ge(v_lo_ready, i - 1)
                wait_slot(V0 + i)
                for t in range(2):
                    last = project_rows(V0 + i, i % 2, t)
                last.then_inc(slot_done, 1)
                transposes(3, i - 2)
            pe.wait_ge(v_lo_ready, 3)
            wide_slot(KQ0, 0, hidA)
            pe.wait_ge(v_lo_ready, 4)
            pe.wait_ge(h_lo_ready, step4(3, 1, 1))
            wide_slot(KQ0 + 1, 1, hidB)

            def scores(h):
                e, par = h % 2, h // 2 % 2
                pe.wait_ge(kq_lo_ready, 2 * (h // 2) + 2)
                if h >= 2:
                    pe.wait_ge(mix_lo_ready, KD // 2 + h - 1)
                K = (kq_hi[:, par, 0, 256 * e:256 * e + 256], kq_lo[:, par, 0, 256 * e:256 * e + 256])
                Q = (kq_hi[:, par, 1, 256 * e:256 * e + 256], kq_lo[:, par, 1, 256 * e:256 * e + 256])
                split_matmul(tr[e][:, 0:P], ([q[:, 0:P] for q in Q], [k[:, 0:P] for k in K]), True, True)
                split_matmul(tr[e][:, P:3 * P], ([q[:, P:2 * P] for q in Q], K), True, True).then_inc(scores_ready, 1)

            def transpose_probs(h):
                e = h % 2
                pe.wait_ge(probs_ready, 2 * h + 2)
                for c in range(3):
                    last = pe.transpose(tr[e][:, P * c:P * c + P], logits[:, e, P * c:P * c + P], ident[:])
                last.then_inc(probs_T, 1)

            def weigh(h):
                e = h % 2
                pe.wait_ge(pt_lo_ready, h + 1)
                V = [[v[:, t, P * h:P * h + P] for v in (v_hi, v_lo)] for t in range(2)]
                split_matmul(tr[e][:, 0:256], (V[0], (pt_hi[:, e, 0:256], pt_lo[:, e, 0:256])), True, False)
                split_matmul(tr[e][:, P:256], (V[1], (pt_hi[:, e, 256:384], pt_lo[:, e, 256:384])),
                             False, True).then_inc(heads_out, 1)

            for p in range(NH // 2 - 1):
                sK, sQ = KQ0 + 2 * p + 2, KQ0 + 2 * p + 3
                wait_slot(sK)
                pe.wait_ge(kq_lo_ready, 2 * p + 1)
                project(sK, 0, hidA, 0)
                scores(2 * p)
                scores(2 * p + 1)
                project(sK, 0, hidA, 1).then_inc(slot_done, 1)
                wait_slot(sQ)
                project(sQ, 1, hidB, 0)
                transpose_probs(2 * p)
                transpose_probs(2 * p + 1)
                project(sQ, 1, hidB, 1).then_inc(slot_done, 1)
                weigh(2 * p)
                weigh(2 * p + 1)
            p = NH // 2 - 1
            wait_slot(O0)
            pe.wait_ge(x_new, 8)
            pe.wait_ge(mix_lo_ready, KD // 2 + 2)
            for e in range(2):
                accumulate(O0, mix_pair(0), 0, e, first=(e == 0))
            scores(2 * p)
            scores(2 * p + 1)
            for e in range(2):
                last = accumulate(O0, mix_pair(0), 1, e, first=(e == 0))
            last.then_inc(slot_done, 1)
            wait_slot(O0 + 1)
            pe.wait_ge(mix_lo_ready, KD // 2 + 4)
            for e in range(2):
                accumulate(O0 + 1, mix_pair(1), 0, e)
            transpose_probs(2 * p)
            transpose_probs(2 * p + 1)
            for e in range(2):
                last = accumulate(O0 + 1, mix_pair(1), 1, e)
            last.then_inc(slot_done, 1)
            weigh(2 * p)
            weigh(2 * p + 1)
            finish(O0 + 2, mix_pair(2), (mix_lo_ready, KD // 2 + 6), mix_pair(3), (mix_lo_ready, KD // 2 + 8), 4)

            ffn(1, 4, 5)


_INS = ["x", "norm_mix", "norm_ffn", "ffn_w_up", "ffn_conv", "ffn_conv_b", "ffn_w_down", "a_w_in", "a_conv",
        "a_w_out", "kv_norm", "w_kv", "b_w_q", "b_w_o", "final_norm"]


def kernel(**inputs):
    import numpy as np
    import concourse.bacc as bacc
    from concourse.bass_utils import run_bass_kernel_spmd

    nc = bacc.Bacc("TRN2", target_bir_lowering=False, num_devices=1)
    arrays, args = {}, []
    for name in _INS:
        a = np.ascontiguousarray(inputs[name])
        arrays[f"in_{name}"] = a
        args.append(nc.dram_tensor(f"in_{name}", a.shape, mybir.dt.from_np(a.dtype), kind="ExternalInput").ap())
    args.append(nc.dram_tensor("out", arrays["in_x"].shape, F32, kind="ExternalOutput").ap())
    build(nc, *args)
    return run_bass_kernel_spmd(nc, [arrays], core_ids=[0]).results[0]["out"]
```

```python
from contextlib import ExitStack

import concourse.bass as bass
from concourse import mybir

F32 = mybir.dt.float32
F32R = mybir.dt.float32r
ALU = mybir.AluOpType
ACT = mybir.ActivationFunctionType
AX_X = mybir.AxisListType.X

P = 128
EPS = 1e-6
RAW = 6
SPLIT = 3
MASKED = -1e30


def build(nc, x, norm_mix, norm_ffn, ffn_w_up, ffn_conv, ffn_conv_b, ffn_w_down,
          a_w_in, a_conv, a_w_out, kv_norm, w_kv, b_w_q, b_w_o, final_norm, out):
    _, S, D = x.shape
    F = ffn_conv.shape[2]
    KD = D // P
    NH = D // P
    TAPS = ffn_conv.shape[1]
    UNITS = F // (2 * P)
    FT = F // P
    COLS = KD * 256
    SCALE = float(P) ** -0.5
    SLOPE = [2.0 ** (-8.0 * (h + 1) / NH) for h in range(NH)]
    assert S == 2 * P and D == 1024 and UNITS * 2 * P == F and COLS == 2 * D and UNITS % 2 == 1

    A_IN, A_B, A_OUT = 0, KD, KD + KD // 2
    FFN = [A_OUT + KD // 2, 0]
    V0 = FFN[0] + 3 * UNITS
    KQ0 = V0 + KD // 2
    O0 = KQ0 + KD
    FFN[1] = O0 + KD // 2
    SLOTS = FFN[1] + 3 * UNITS

    TURN = 2 * 3
    assert TURN % RAW == 0 and TURN % SPLIT == 0
    TURNS = (UNITS - 3) // 2

    def gate_slot(l, j):
        return FFN[l] if j == 0 else FFN[l] + 3 * j - 1

    def after(n, turn, step):
        return n if turn is None else n + step * turn

    def rows(w):
        return w.rearrange("(k p) n -> p k n", p=P)

    in_rows, aout_rows = rows(a_w_in[0]), rows(a_w_out[0])
    kv_rows, q_rows, o_rows = rows(w_kv), rows(b_w_q[0]), rows(b_w_o[0])
    up_rows = [rows(ffn_w_up[l]) for l in range(2)]
    down_rows = [rows(ffn_w_down[l]) for l in range(2)]
    x_rows = x[0].rearrange("(t p) n -> p t n", p=P)
    out_rows = out[0].rearrange("(t p) n -> p t n", p=P)

    with ExitStack() as ctx:
        def sb(name, shape, dt=F32):
            return ctx.enter_context(nc.sbuf_tensor(name, shape, dt))

        def sem(name):
            return ctx.enter_context(nc.semaphore(name))

        raw = sb("raw", [P, RAW, COLS])
        w_hi = sb("w_hi", [P, SPLIT, COLS], F32R)
        w_lo = sb("w_lo", [P, SPLIT, COLS], F32R)
        xs = sb("xs", [P, 2, D])
        hA_hi = sb("hA_hi", [P, KD, S], F32R)
        hA_lo = sb("hA_lo", [P, KD, S], F32R)
        hB_hi = sb("hB_hi", [P, KD, S], F32R)
        hB_lo = sb("hB_lo", [P, KD, S], F32R)
        mix_hi = sb("mix_hi", [P, KD, S], F32R)
        mix_lo = sb("mix_lo", [P, KD, S], F32R)
        v_hi = sb("v_hi", [P, 2, D], F32R)
        v_lo = sb("v_lo", [P, 2, D], F32R)
        kq_hi = sb("kq_hi", [P, 2, 2, 512], F32R)
        kq_lo = sb("kq_lo", [P, 2, 2, 512], F32R)
        pt_hi = sb("pt_hi", [P, 2, 384], F32R)
        pt_lo = sb("pt_lo", [P, 2, 384], F32R)
        scratch = sb("scratch", [P, 2 * D])
        gain = sb("gain", [P, D])
        dist = sb("dist", [P, 384])
        ident = sb("ident", [P, P])
        ones = sb("ones", [1, P])
        par_rows = sb("par_rows", [P, 3, P])
        a_par = sb("a_par", [P, TAPS * KD])
        f_par = sb("f_par", [P, 2, (TAPS + 1) * FT])
        sumsq = sb("sumsq", [P, 2, 2])
        msq = sb("msq", [P, 2, 2])
        rstd = sb("rstd", [P, 2])
        minus_half = sb("minus_half", [P, 1])
        mx = sb("mx", [P, 2, 2])
        nbias = sb("nbias", [P, 2, 2])
        psums = sb("psums", [P, 2, 2])
        rinv = sb("rinv", [P, 2, 2])

        normed = scratch[:].rearrange("p (t n) -> p t n", t=2)
        conv_out = scratch[:].rearrange("p (f n) -> p f n", f=KD)
        glu = scratch[:, 0:1024].rearrange("p (b e n) -> p b e n", b=2, e=2)
        logits = scratch[:, 0:768].rearrange("p (e n) -> p e n", e=2)
        opening = scratch[:, 1024:2048].rearrange("p (b n) -> p b n", b=2)
        c_sb = gain[:, 0:512]
        cx = gain[:, 512:1024].rearrange("p (e n) -> p e n", e=2)
        act_hi = kq_hi[:].rearrange("p a b n -> p (a b n)")[:, 0:1024].rearrange("p (b e n) -> p b e n", b=2, e=2)
        act_lo = kq_lo[:].rearrange("p a b n -> p (a b n)")[:, 0:1024].rearrange("p (b e n) -> p b e n", b=2, e=2)

        bank = [ctx.enter_context(nc.psum_tensor(f"proj{i}", [P, 512], F32)) for i in range(2)]
        acc = [[ctx.enter_context(nc.psum_tensor(f"acc{t}{h}", [P, 512], F32)) for h in range(2)] for t in range(2)]
        tr = [ctx.enter_context(nc.psum_tensor(f"tr{i}", [P, 512], F32)) for i in range(2)]

        landed = [sem(f"landed{r}") for r in range(RAW)]
        x0_in = [sem("x0_in_a"), sem("x0_in_b")]
        x1_in = sem("x1_in")
        gain_in = sem("gain_in")
        gain0_spread = sem("gain0_spread")
        gained = sem("gained")
        par_in = sem("par_in")
        consts = sem("consts")
        zeroed = sem("zeroed")
        w_hi_ready = sem("w_hi_ready")
        w_lo_ready = sem("w_lo_ready")
        ahead_hi = sem("ahead_hi")
        ahead_lo = sem("ahead_lo")
        slot_done = sem("slot_done")
        acc_done = sem("acc_done")
        par_T = sem("par_T")
        par_ready = sem("par_ready")
        x_new = sem("x_new")
        squared = sem("squared")
        ms_part = sem("ms_part")
        ms_full = sem("ms_full")
        rstd_ready = sem("rstd_ready")
        normed_ready = sem("normed_ready")
        x_T = sem("x_T")
        opening_copied = sem("opening_copied")
        opening_T = sem("opening_T")
        first_landed = sem("first_landed")
        first_hi = sem("first_hi")
        first_lo = sem("first_lo")
        h_hi_ready = sem("h_hi_ready")
        h_lo_ready = sem("h_lo_ready")
        c_copied = sem("c_copied")
        cx_ready = sem("cx_ready")
        a_conv_op = sem("a_conv_op")
        a_conv_done = sem("a_conv_done")
        gated = sem("gated")
        mix_hi_ready = sem("mix_hi_ready")
        mix_lo_ready = sem("mix_lo_ready")
        tap0 = sem("tap0")
        conv_op = sem("conv_op")
        silu_done = sem("silu_done")
        act_full = sem("act_full")
        act_hi_ready = sem("act_hi_ready")
        act_lo_ready = sem("act_lo_ready")
        v_hi_ready = sem("v_hi_ready")
        v_lo_ready = sem("v_lo_ready")
        kq_hi_ready = sem("kq_hi_ready")
        kq_lo_ready = sem("kq_lo_ready")
        scores_ready = sem("scores_ready")
        logits_ready = sem("logits_ready")
        max_ready = sem("max_ready")
        nbias_ready = sem("nbias_ready")
        exp_ready = sem("exp_ready")
        rinv_ready = sem("rinv_ready")
        probs_ready = sem("probs_ready")
        probs_T = sem("probs_T")
        pt_hi_ready = sem("pt_hi_ready")
        pt_lo_ready = sem("pt_lo_ready")
        heads_out = sem("heads_out")
        stored = sem("stored")

        AHEAD = [FFN[0] + 1, V0 + 1, FFN[1] + 1]

        def split_slot(s):
            if s in AHEAD:
                return [h[:].rearrange("p k n -> p (k n)") for h in (hB_hi, hB_lo)]
            return w_hi[:, s % SPLIT, :], w_lo[:, s % SPLIT, :]

        STAT = [0, 1, 2, 2, 3, 4]
        GAIN = [norm_mix[0], norm_ffn[0], kv_norm, norm_mix[1], norm_ffn[1], final_norm]
        HID = [(hA_hi, hA_lo), (hA_hi, hA_lo), (hA_hi, hA_lo), (hB_hi, hB_lo), (hA_hi, hA_lo)]
        LAST = [A_OUT + KD // 2 - 1, FFN[0] + 3 * UNITS - 1, O0 + KD // 2 - 1, FFN[1] + 3 * UNITS - 1]

        def step4(n, t, h):
            return 4 * n + 2 * t + h + 1

        block = ctx.enter_context(nc.Block())

        @block.sync
        def _(sp):
            def load(s, src, turn=None):
                if s >= RAW:
                    sp.wait_ge(w_lo_ready, after(s - RAW + 1, turn, TURN))
                sp.dma_start(raw[:, s % RAW, :].rearrange("p (k n) -> p k n", k=src.shape[1]), src).then_inc(landed[s % RAW], 16)

            def wide(w, c0):
                return w[:, :, bass.ds(c0, 256)]

            def ffn_loads(l, j, turn=None):
                s, at = gate_slot(l, j), after(j, turn, 2)
                load(s, wide(up_rows[l], at * 256), turn)
                load(s + 1, wide(up_rows[l], at * 256 + F), turn)
                if j:
                    load(s + 2, down_rows[l][:, bass.ds(at * 2 - 2, 2), :], turn)

            def ffn_stream(l):
                ffn_loads(l, 0)
                with sp.Fori(0, TURNS) as turn:
                    ffn_loads(l, 1, turn)
                    ffn_loads(l, 2, turn)
                for j in (UNITS - 2, UNITS - 1):
                    ffn_loads(l, j)
                load(FFN[l] + 3 * UNITS - 1, down_rows[l][:, 2 * UNITS - 2:2 * UNITS, :])

            for h in range(2):
                sp.dma_start(xs[:, 0, 512 * h:512 * h + 512], x_rows[:, 0, 512 * h:512 * h + 512]).then_inc(x0_in[h], 16)
            sp.dma_start(xs[:, 1, :], x_rows[:, 1, :]).then_inc(x1_in, 16)
            halves = raw[:, 0, :].rearrange("p (g k n) -> p g k n", g=2, n=256)
            for g, landing in enumerate((first_landed, landed[0])):
                sp.dma_start(halves[:, g], in_rows[:, 4 * g:4 * g + 4, D:D + 256]).then_inc(landing, 16)
            load(1, wide(in_rows, 2 * D))
            load(2, wide(in_rows, D + 256))
            sp.dma_start(par_rows[0:TAPS * KD, 0, :], a_conv[0].rearrange("t (k n) -> (t k) n", n=P)).then_inc(par_in, 16)
            for l in range(2):
                sp.dma_start(par_rows[0:TAPS * FT, 1 + l, :],
                             ffn_conv[l].rearrange("t (k n) -> (t k) n", n=P)).then_inc(par_in, 16)
                sp.dma_start(par_rows[TAPS * FT:(TAPS + 1) * FT, 1 + l, :],
                             ffn_conv_b[l].rearrange("(k n) -> k n", n=P)).then_inc(par_in, 16)
            load(3, wide(in_rows, 2 * D + 256))
            for i in range(2, KD // 2):
                load(A_IN + 2 * i, wide(in_rows, D + 256 * i))
                load(A_IN + 2 * i + 1, wide(in_rows, 2 * D + 256 * i))
            for i in range(KD // 2):
                load(A_B + i, wide(in_rows, 256 * i))
            for i in range(KD // 2):
                load(A_OUT + i, aout_rows[:, 2 * i:2 * i + 2, :])
            ffn_stream(0)
            for i in range(KD // 2):
                load(V0 + i, wide(kv_rows, D + 256 * i))
            for i in range(KD // 2):
                load(KQ0 + 2 * i, wide(kv_rows, 256 * i))
                load(KQ0 + 2 * i + 1, wide(q_rows, 256 * i))
            for i in range(KD // 2):
                load(O0 + i, o_rows[:, 2 * i:2 * i + 2, :])
            ffn_stream(1)
            for t in range(2):
                for h in range(2):
                    sp.wait_ge(normed_ready, step4(5, t, h))
                    sp.dma_start(out_rows[:, t, 512 * h:512 * h + 512],
                                 normed[:, t, 512 * h:512 * h + 512]).then_inc(stored, 16)
            sp.wait_ge(stored, 64)

        @block.gpsimd
        def _(pool):

            def root(z, t):
                pool.wait_ge(ms_full, 2 * z + t + 1)
                pool.tensor_tensor(rstd[:, t:t + 1], msq[:, t, 1:2], minus_half[:], ALU.pow).then_inc(rstd_ready, 1)

            pool.memset(ident[:], 0.0).then_inc(zeroed, 1)
            pool.memset(minus_half[:], -0.5).then_inc(zeroed, 1)
            pool.memset(ones[:], 1.0).then_inc(zeroed, 1)
            pool.wait_ge(zeroed, 3)
            pool.affine_select(out=ident[:], in_=ident[:], compare_op=ALU.not_equal, fill=1.0, base=0,
                               pattern=[[-1, P]], channel_multiplier=1).then_inc(consts, 1)
            pool.iota(dist[:, 0:128], pattern=[[1, 128]], base=0, channel_multiplier=-1,
                      allow_small_or_imprecise_dtypes=True).then_inc(zeroed, 1)
            pool.iota(dist[:, 128:384], pattern=[[1, 256]], base=-P, channel_multiplier=-1,
                      allow_small_or_imprecise_dtypes=True).then_inc(zeroed, 1)
            pool.wait_ge(zeroed, 5)
            pool.affine_select(out=dist[:, 0:128], in_=dist[:, 0:128], compare_op=ALU.is_ge, fill=MASKED, base=0,
                               pattern=[[-1, 128]], channel_multiplier=1).then_inc(consts, 1)
            pool.affine_select(out=dist[:, 128:384], in_=dist[:, 128:384], compare_op=ALU.is_ge, fill=MASKED, base=P,
                               pattern=[[-1, 256]], channel_multiplier=1).then_inc(consts, 1)
            root(0, 0)
            root(0, 1)
            for z in range(1, 5):
                root(z, 0)
                root(z, 1)

        @block.scalar
        def _(act):
            def hi(s, turn=None):
                if s >= SLOTS or s in AHEAD:
                    return
                act.wait_ge(landed[s % RAW], after(16 * (s // RAW + 1), turn, 16))
                if s >= SPLIT:
                    act.wait_ge(slot_done, after(s - SPLIT + 1, turn, TURN))
                act.activation(split_slot(s)[0], raw[:, s % RAW, :], ACT.Copy).then_inc(w_hi_ready, 2 if s + 1 in AHEAD else 1)

            def hi_ahead(o):
                s = AHEAD[o]
                act.wait_ge(landed[s % RAW], 16 * (s // RAW + 1))
                if o == 2:
                    act.wait_ge(slot_done, O0)
                act.activation(split_slot(s)[0], raw[:, s % RAW, :], ACT.Copy).then_inc(ahead_hi, 1)

            def square(z, t, h):
                part = xs[:, t, 512 * h:512 * h + 512]
                if z:
                    act.wait_ge(x_new, step4(z - 1, t, h))
                else:
                    act.wait_ge(*((x1_in, 16) if t else (x0_in[h], 16)))
                    if t or h:
                        act.wait_ge(squared, 2 * t + h)
                act.activation((acc[t][h] if z else acc[0][0])[:], part, ACT.Square,
                               accum_out=sumsq[:, t, h:h + 1]).then_inc(squared, 1)

            def h_hi(n, t, h):
                act.wait_ge(x_T, step4(n, t, h))
                act.activation(HID[n][0][:, 4 * h:4 * h + 4, P * t:P * t + P],
                               tr[h][:].rearrange("p (k n) -> p k n", k=4), ACT.Copy).then_inc(h_hi_ready, 1)

            def load_gain(n):
                if n > 1:
                    act.wait_ge(normed_ready, step4(n - 1, 1, 1))
                else:
                    act.wait_ge(a_conv_done, KD)
                act.dma_start(gain[:], GAIN[n].rearrange("(a n) -> a n", a=1).to_broadcast([P, D])).then_inc(gain_in, 16)

            def boundary(r, n):
                for h in range(2):
                    square(r + 1, 0, h)
                if n < 5:
                    for h in range(2):
                        h_hi(n, 0, h)
                for h in range(2):
                    square(r + 1, 1, h)
                if n < 5:
                    for h in range(2):
                        h_hi(n, 1, h)
                    load_gain(n + 1)

            def copy_opening(s, b, o):
                act.wait_ge(slot_done, s + b + 1)
                act.activation(opening[:, b, :], bank[b][:], ACT.Copy).then_inc(opening_copied, 1)

            def unit(l, j, turn=None):
                s, U = gate_slot(l, j), l * UNITS + j
                g = glu[:, U % 2]
                gate = bank[0] if j else tr[0]
                if j:
                    act.wait_ge(slot_done, after(s + 1, turn, TURN))
                else:
                    hi(s + 2)
                    copy_opening(s, 0, l + 1)
                    hi(s + 3)
                    copy_opening(s, 1, l + 1)
                    act.wait_ge(opening_T, 2 * (l + 1) + 1)
                for e in range(2):
                    f = after(2 * j + e, turn, 4)
                    ins = act.activation(g[:, e, :], gate[:, 256 * e:256 * e + 256], ACT.Identity,
                                         bias=f_par[:, l, bass.ds(f + TAPS * FT, 1)],
                                         scale=f_par[:, l, bass.ds(f + (TAPS - 1) * FT, 1)])
                ins.then_inc(tap0, 1)
                hi(s + 3 if j else s + 4, turn)
                act.wait_ge(conv_op, after(4 * U + 4, turn, 8))
                act.activation(g, g, ACT.Silu).then_inc(silu_done, 1)
                act.wait_ge(act_full, after(U + 1, turn, 2))
                act.activation(act_hi[:, U % 2], g, ACT.Copy).then_inc(act_hi_ready, 1)
                if j:
                    hi(s + 4, turn)
                    if j < UNITS - 1:
                        hi(s + 5, turn)

            def ffn(l):
                unit(l, 0)
                with act.Fori(0, TURNS) as turn:
                    unit(l, 1, turn)
                    unit(l, 2, turn)
                unit(l, UNITS - 2)
                if l == 0:
                    hi_ahead(1)
                unit(l, UNITS - 1)

            def exp(h):
                e = h % 2
                act.wait_ge(nbias_ready, h + 1)
                for t, cols in ((0, slice(0, 128)), (1, slice(128, 384))):
                    act.activation(logits[:, e, cols], logits[:, e, cols], ACT.Exp, bias=nbias[:, e, t:t + 1],
                                   scale=SCALE, accum_out=psums[:, e, t:t + 1]).then_inc(exp_ready, 1)

            def kq(i):
                act.wait_ge(slot_done, KQ0 + i + 1)
                act.activation(kq_hi[:, i // 2 % 2, i % 2, :], bank[i % 2][:], ACT.Copy).then_inc(kq_hi_ready, 1)

            def v(i):
                act.wait_ge(slot_done, V0 + i + 1)
                act.activation(v_hi[:, :, 256 * i:256 * i + 256],
                               bank[i % 2][:].rearrange("p (t n) -> p t n", t=2), ACT.Copy).then_inc(v_hi_ready, 1)

            def first_half_hi():
                act.wait_ge(first_landed, 16)
                act.activation(w_hi[:, 0, 0:COLS // 2], raw[:, 0, 0:COLS // 2], ACT.Copy).then_inc(first_hi, 1)

            act.dma_start(gain[0:1, :], GAIN[0].rearrange("(a n) -> a n", a=1)).then_inc(gain_in, 16)
            for t in range(2):
                for h in range(2):
                    square(0, t, h)
            first_half_hi()
            for h in range(2):
                h_hi(0, 0, h)
            act.wait_ge(landed[0], 16)
            act.activation(w_hi[:, 0, COLS // 2:], raw[:, 0, COLS // 2:], ACT.Copy).then_inc(w_hi_ready, 1)
            hi(1)
            for h in range(2):
                h_hi(0, 1, h)
            hi(2)
            for i in range(KD // 2):
                if i == 0:
                    for b in range(2):
                        copy_opening(A_IN, b, 0)
                        hi(3 + b)
                    act.wait_ge(opening_T, 1)
                else:
                    act.wait_ge(slot_done, A_IN + 2 * i + 1)
                    act.wait_ge(cx_ready, i)
                act.activation(c_sb, (bank[0] if i else tr[0])[:], ACT.Copy).then_inc(c_copied, 1)
                if i:
                    hi(2 * i + 3)
                    hi(2 * i + 4)

            def mixed(i):
                act.wait_ge(gated, i + 1)
                act.activation(mix_hi[:, 2 * i:2 * i + 2, :], conv_out[:, 2 * i:2 * i + 2, :],
                               ACT.Copy).then_inc(mix_hi_ready, 1)

            for i in range(KD // 2 - 1):
                mixed(i)
                hi(A_B + i + 3)
            hi_ahead(0)
            load_gain(1)
            mixed(KD // 2 - 1)
            hi(A_OUT + 2)
            hi(A_OUT + 3)
            hi(A_OUT + 4)
            boundary(0, 1)
            ffn(0)
            boundary(1, 2)

            hi(V0 + 2)
            for i in range(KD // 2):
                v(i)
                if i >= 2:
                    for h in range(2):
                        h_hi(3, i - 2, h)
                if i == 2:
                    load_gain(4)
                hi(V0 + i + 3)
            kq(0)
            hi(KQ0 + 3)
            for p in range(NH // 2):
                kq(2 * p + 1)
                hi(KQ0 + 2 * p + 4)
                if p == NH // 2 - 1:
                    hi_ahead(2)
                exp(2 * p)
                exp(2 * p + 1)
                if p < NH // 2 - 1:
                    kq(2 * p + 2)
                for e in range(2):
                    act.wait_ge(probs_T, 2 * p + e + 1)
                    act.activation(pt_hi[:, e, :], tr[e][:, 0:384], ACT.Copy).then_inc(pt_hi_ready, 1)
                hi(KQ0 + 2 * p + 5)
                for e in range(2):
                    act.wait_ge(heads_out, 2 * p + e + 1)
                    act.activation(mix_hi[:, 2 * p + e, :], tr[e][:, 0:256], ACT.Copy).then_inc(mix_hi_ready, 1)
            hi(O0 + 4)
            boundary(2, 4)
            ffn(1)
            boundary(3, 5)

        @block.vector
        def _(dve):
            def lo(s, turn=None):
                if s >= SLOTS or s in AHEAD:
                    return
                dve.wait_ge(w_hi_ready, after(s + 1, turn, TURN))
                whi, wlo = split_slot(s)
                dve.tensor_tensor(wlo, raw[:, s % RAW, :], whi.bitcast(F32),
                                  ALU.subtract).then_inc(w_lo_ready, 2 if s + 1 in AHEAD else 1)

            def lo_ahead(o):
                dve.wait_ge(ahead_hi, o + 1)
                whi, wlo = split_slot(AHEAD[o])
                dve.tensor_tensor(wlo, raw[:, AHEAD[o] % RAW, :], whi.bitcast(F32), ALU.subtract).then_inc(ahead_lo, 1)

            def residual(r, t, h):
                dve.wait_ge(*((slot_done, LAST[r] + 1) if t and h else (acc_done, 3 * r + 2 * t + h + 1)))
                part = xs[:, t, 512 * h:512 * h + 512]
                dve.tensor_tensor(part, part, acc[t][h][:], ALU.add).then_inc(x_new, 1)

            def mean_square(z, t):
                dve.wait_ge(squared, step4(z, t, 0))
                dve.tensor_scalar(msq[:, t, 0:1], sumsq[:, t, 0:1], 1.0 / D, EPS, ALU.mult, ALU.add).then_inc(ms_part, 1)
                dve.wait_ge(squared, step4(z, t, 1))
                dve.wait_ge(ms_part, 2 * z + t + 1)
                dve.tensor_scalar(msq[:, t, 1:2], sumsq[:, t, 1:2], 1.0 / D, msq[:, t, 0:1],
                                  ALU.mult, ALU.add).then_inc(ms_full, 1)

            def apply_gain(n, t, h):
                dve.wait_ge(gain_in, 16 * (n + 1))
                dve.wait_ge(x_new, step4(STAT[n] - 1, t, h))
                cols = slice(512 * h, 512 * h + 512)
                dve.tensor_tensor(normed[:, t, cols], xs[:, t, cols], gain[:, cols], ALU.mult).then_inc(gained, 1)

            def normalise(n, t):
                dve.wait_ge(rstd_ready, 2 * STAT[n] + t + 1)
                for h in range(2):
                    cols = slice(512 * h, 512 * h + 512)
                    if n in (0, 3):
                        dve.wait_ge(*((gain_in, 16 * 4) if n else (gain0_spread, h + 1)))
                        dve.scalar_tensor_tensor(out=normed[:, t, cols], in0=xs[:, t, cols], scalar=rstd[:, t:t + 1],
                                                 in1=gain[:, cols] if n else acc[1][h][:],
                                                 op0=ALU.mult, op1=ALU.mult).then_inc(normed_ready, 1)
                    else:
                        dve.wait_ge(gained, step4(STAT[n] - 1, t, h))
                        dve.tensor_scalar(normed[:, t, cols], normed[:, t, cols], rstd[:, t:t + 1], None,
                                          ALU.mult).then_inc(normed_ready, 1)

            def h_lo_half(n, t, h):
                dve.wait_ge(h_hi_ready, step4(n, t, h))
                dve.tensor_tensor(HID[n][1][:, 4 * h:4 * h + 4, P * t:P * t + P],
                                  tr[h][:].rearrange("p (k n) -> p k n", k=4),
                                  HID[n][0][:, 4 * h:4 * h + 4, P * t:P * t + P].bitcast(F32),
                                  ALU.subtract).then_inc(h_lo_ready, 1)

            def h_lo(n, t):
                for h in range(2):
                    h_lo_half(n, t, h)

            def boundary(r, n):
                residual(r, 0, 0)
                residual(r, 0, 1)
                apply_gain(n, 0, 0)
                mean_square(r + 1, 0)
                apply_gain(n, 0, 1)
                normalise(n, 0)
                residual(r, 1, 0)
                if n < 5:
                    h_lo(n, 0)
                residual(r, 1, 1)
                apply_gain(n, 1, 0)
                mean_square(r + 1, 1)
                apply_gain(n, 1, 1)
                normalise(n, 1)
                if n < 5:
                    h_lo(n, 1)

            def unit(l, j, turn=None):
                s, U = gate_slot(l, j), l * UNITS + j
                g = glu[:, U % 2]
                gate, up = bank if j else tr
                if j == 0:
                    lo(s + 2)
                    lo(s + 3)
                dve.wait_ge(tap0, after(U + 1, turn, 2))
                for back in (1, 2):
                    for e in range(2):
                        if back == 2:
                            dve.wait_ge(conv_op, after(4 * U + e + 1, turn, 8))
                        f = after(2 * j + e, turn, 4)
                        dst = g[:, e, back:S]
                        dve.scalar_tensor_tensor(out=dst, in0=gate[:, 256 * e:256 * e + S - back],
                                                 scalar=f_par[:, l, bass.ds(f + (TAPS - 1 - back) * FT, 1)],
                                                 in1=dst, op0=ALU.mult, op1=ALU.add).then_inc(conv_op, 1)
                lo(s + 3 if j else s + 4, turn)
                if j:
                    dve.wait_ge(slot_done, after(s + 2, turn, TURN))
                else:
                    dve.wait_ge(opening_T, 2 * (l + 1) + 2)
                dve.wait_ge(silu_done, after(U + 1, turn, 2))
                dve.tensor_tensor(g, g, up[:].rearrange("p (e n) -> p e n", e=2), ALU.mult).then_inc(act_full, 1)
                dve.wait_ge(act_hi_ready, after(U + 1, turn, 2))
                dve.tensor_tensor(act_lo[:, U % 2], g, act_hi[:, U % 2].bitcast(F32),
                                  ALU.subtract).then_inc(act_lo_ready, 1)
                if j:
                    lo(s + 4, turn)
                    if j < UNITS - 1:
                        lo(s + 5, turn)

            def ffn(l):
                unit(l, 0)
                with dve.Fori(0, TURNS) as turn:
                    unit(l, 1, turn)
                    unit(l, 2, turn)
                unit(l, UNITS - 2)
                if l == 0:
                    lo_ahead(1)
                unit(l, UNITS - 1)

            def conv_a(i):
                if i:
                    dve.wait_ge(slot_done, A_IN + 2 * i + 2)
                else:
                    dve.wait_ge(opening_T, 2)
                dve.wait_ge(c_copied, i + 1)
                if i:
                    dve.wait_ge(a_conv_done, 2 * i)
                dve.tensor_tensor(cx, c_sb.rearrange("p (e n) -> p e n", e=2),
                                  (bank[1] if i else tr[1])[:].rearrange("p (e n) -> p e n", e=2),
                                  ALU.mult).then_inc(cx_ready, 1)
                dve.wait_ge(cx_ready, i + 1)
                for e in range(2):
                    f = 2 * i + e
                    tap = [a_par[:, c * KD + f:c * KD + f + 1] for c in range(TAPS)]
                    dve.tensor_scalar(conv_out[:, f, :], cx[:, e, :], tap[2], None, ALU.mult).then_inc(a_conv_op, 1)
                    dve.wait_ge(a_conv_op, 2 * f + 1)
                    dve.scalar_tensor_tensor(out=conv_out[:, f, 1:S], in0=cx[:, e, 0:S - 1], scalar=tap[1],
                                             in1=conv_out[:, f, 1:S], op0=ALU.mult, op1=ALU.add).then_inc(a_conv_op, 1)
                    dve.wait_ge(a_conv_op, 2 * f + 2)
                    dve.scalar_tensor_tensor(out=conv_out[:, f, 2:S], in0=cx[:, e, 0:S - 2], scalar=tap[0],
                                             in1=conv_out[:, f, 2:S], op0=ALU.mult, op1=ALU.add).then_inc(a_conv_done, 1)

            def gate_a(i):
                dve.wait_ge(slot_done, A_B + i + 1)
                dve.wait_ge(a_conv_done, 2 * i + 2)
                dst = conv_out[:, 2 * i:2 * i + 2, :]
                dve.tensor_tensor(dst, dst, bank[i % 2][:].rearrange("p (e n) -> p e n", e=2), ALU.mult).then_inc(gated, 1)
                dve.wait_ge(mix_hi_ready, i + 1)
                dve.tensor_tensor(mix_lo[:, 2 * i:2 * i + 2, :], dst, mix_hi[:, 2 * i:2 * i + 2, :].bitcast(F32),
                                  ALU.subtract).then_inc(mix_lo_ready, 1)

            def kq(i):
                dve.wait_ge(kq_hi_ready, i + 1)
                dve.tensor_tensor(kq_lo[:, i // 2 % 2, i % 2, :], bank[i % 2][:],
                                  kq_hi[:, i // 2 % 2, i % 2, :].bitcast(F32), ALU.subtract).then_inc(kq_lo_ready, 1)

            def v(i):
                dve.wait_ge(v_hi_ready, i + 1)
                cols = slice(256 * i, 256 * i + 256)
                dve.tensor_tensor(v_lo[:, :, cols], bank[i % 2][:].rearrange("p (t n) -> p t n", t=2),
                                  v_hi[:, :, cols].bitcast(F32), ALU.subtract).then_inc(v_lo_ready, 1)

            def row_max(h):
                e = h % 2
                dve.wait_ge(scores_ready, h + 1)
                dve.scalar_tensor_tensor(out=logits[:, e, :], in0=dist[:], scalar=SLOPE[h] / SCALE, in1=tr[e][:, 0:384],
                                         op0=ALU.mult, op1=ALU.add).then_inc(logits_ready, 1)
                dve.wait_ge(logits_ready, h + 1)
                dve.reduce_max(mx[:, e, 0:1], logits[:, e, 0:128], AX_X).then_inc(max_ready, 1)
                dve.reduce_max(mx[:, e, 1:2], logits[:, e, 128:384], AX_X).then_inc(max_ready, 1)
                dve.wait_ge(max_ready, 2 * h + 2)
                dve.tensor_scalar(nbias[:, e, :], mx[:, e, :], -SCALE, None, ALU.mult).then_inc(nbias_ready, 1)

            def normal_probs(h):
                e = h % 2
                dve.wait_ge(exp_ready, 2 * h + 2)
                dve.reciprocal(rinv[:, e, :], psums[:, e, :]).then_inc(rinv_ready, 1)
                dve.wait_ge(rinv_ready, h + 1)
                for t, cols in ((0, slice(0, 128)), (1, slice(128, 384))):
                    dve.tensor_scalar(logits[:, e, cols], logits[:, e, cols], rinv[:, e, t:t + 1], None,
                                      ALU.mult).then_inc(probs_ready, 1)

            mean_square(0, 0)
            normalise(0, 0)
            mean_square(0, 1)
            dve.wait_ge(first_hi, 1)
            dve.tensor_tensor(w_lo[:, 0, 0:COLS // 2], raw[:, 0, 0:COLS // 2], w_hi[:, 0, 0:COLS // 2].bitcast(F32),
                              ALU.subtract).then_inc(first_lo, 1)
            h_lo(0, 0)
            normalise(0, 1)
            dve.wait_ge(w_hi_ready, 1)
            dve.tensor_tensor(w_lo[:, 0, COLS // 2:], raw[:, 0, COLS // 2:], w_hi[:, 0, COLS // 2:].bitcast(F32),
                              ALU.subtract).then_inc(w_lo_ready, 1)
            h_lo(0, 1)
            lo(1)
            lo(2)
            dve.wait_ge(par_T, 1)
            dve.tensor_copy(a_par[:], acc[0][0][:, 0:TAPS * KD]).then_inc(par_ready, 1)
            for l in range(2):
                dve.tensor_copy(f_par[:, l, :], acc[1][l][:, 0:(TAPS + 1) * FT]).then_inc(par_ready, 1)
            dve.wait_ge(par_ready, 3)
            lo(3)
            lo(4)
            for i in range(KD // 2):
                if i:
                    lo(2 * i + 3)
                conv_a(i)
                if i:
                    lo(2 * i + 4)
            for i in range(KD // 2 - 1):
                gate_a(i)
                lo(A_B + i + 3)
            lo_ahead(0)
            gate_a(KD // 2 - 1)
            lo(A_OUT + 2)
            lo(A_OUT + 3)
            lo(A_OUT + 4)
            boundary(0, 1)
            ffn(0)
            boundary(1, 2)

            dve.wait_ge(consts, 3)
            lo(V0 + 2)
            for i in range(KD // 2):
                v(i)
                if i < 2:
                    normalise(3, i)
                else:
                    h_lo(3, i - 2)
                lo(V0 + i + 3)
            kq(0)
            lo(KQ0 + 3)
            for p in range(NH // 2):
                kq(2 * p + 1)
                lo(KQ0 + 2 * p + 4)
                for e in range(2):
                    row_max(2 * p + e)
                for e in range(2):
                    normal_probs(2 * p + e)
                if p < NH // 2 - 1:
                    kq(2 * p + 2)
                for e in range(2):
                    dve.wait_ge(pt_hi_ready, 2 * p + e + 1)
                    dve.tensor_tensor(pt_lo[:, e, :], tr[e][:, 0:384], pt_hi[:, e, :].bitcast(F32),
                                      ALU.subtract).then_inc(pt_lo_ready, 1)
                if p == NH // 2 - 1:
                    lo_ahead(2)
                lo(KQ0 + 2 * p + 5)
                for e in range(2):
                    dve.wait_ge(mix_hi_ready, KD // 2 + 2 * p + e + 1)
                    dve.tensor_tensor(mix_lo[:, 2 * p + e, :], tr[e][:, 0:256], mix_hi[:, 2 * p + e, :].bitcast(F32),
                                      ALU.subtract).then_inc(mix_lo_ready, 1)
            lo(O0 + 4)
            boundary(2, 4)
            ffn(1)
            boundary(3, 5)

        @block.tensor
        def _(pe):
            def split_matmul(dst, parts, first, last):
                (sh, sl), (mh, ml) = parts
                pe.matmul(dst, sh, mh, start=first, stop=False)
                pe.matmul(dst, sh, ml, start=False, stop=False)
                return pe.matmul(dst, sl, mh, start=False, stop=last)

            def wait_slot(s, turn=None):
                if s in AHEAD:
                    pe.wait_ge(ahead_lo, AHEAD.index(s) + 1)
                    return
                pe.wait_ge(w_lo_ready, after(s + 1, turn, TURN))

            def project(s, b, hid, e):
                whi, wlo = split_slot(s)
                for k in range(KD):
                    w = slice(256 * k + P * e, 256 * k + P * e + P)
                    last = split_matmul(bank[b][:, 256 * e:256 * e + S],
                                        ((whi[:, w], wlo[:, w]), (hid[0][:, k, :], hid[1][:, k, :])),
                                        k == 0, k == KD - 1)
                return last

            def project_rows(s, b, t, n=None, halfway=None):
                tok = slice(P * t, P * t + P)
                whi, wlo = split_slot(s)
                for k in range(KD):
                    if halfway and k == KD // 2:
                        halfway()
                    if n is not None and k % 4 == 0:
                        pe.wait_ge(h_lo_ready, step4(n, t, k // 4))
                    if s == 0 and k % 4 == 0 and t == 0:
                        pe.wait_ge(*((w_lo_ready, 1) if k else (first_lo, 1)))
                    w = slice(256 * k, 256 * k + 256)
                    last = split_matmul(bank[b][:, 256 * t:256 * t + 256],
                                        ((hA_hi[:, k, tok], hA_lo[:, k, tok]), (whi[:, w], wlo[:, w])),
                                        k == 0, k == KD - 1)
                return last

            def accumulate(s, left, t, e, first=False):
                ah, al = [part[:, P * t:P * t + P] for part in left[e]]
                wh, wl = [[w[:, s % SPLIT, D * e + 512 * h:D * e + 512 * h + 512] for h in range(2)] for w in (w_hi, w_lo)]
                for h in range(2):
                    pe.matmul(acc[t][h][:], ah, wh[h], start=first, stop=False)
                for h in range(2):
                    pe.matmul(acc[t][h][:], ah, wl[h], start=False, stop=False)
                for h in range(2):
                    last = pe.matmul(acc[t][h][:], al, wh[h], start=False, stop=False)
                return last

            def transposes(n, t):
                for h in range(2):
                    pe.wait_ge(normed_ready, step4(n, t, h))
                    if n or t:
                        pe.wait_ge(h_lo_ready, step4(n, t, h) - 2)
                    for k in range(4):
                        last = pe.transpose(tr[h][:, P * k:P * k + P],
                                            normed[:, t, 512 * h + P * k:512 * h + P * k + P], ident[:])
                    last.then_inc(x_T, 1)

            def accumulate_half(s, left, t, h):
                for e in range(2):
                    act_parts = [part[:, P * t:P * t + P] for part in left[e]]
                    w = slice(D * e + 512 * h, D * e + 512 * h + 512)
                    last = split_matmul(acc[t][h][:], (act_parts, (w_hi[:, s % SPLIT, w], w_lo[:, s % SPLIT, w])),
                                        False, e == 1)
                return last

            def finish(sA, leftA, ready_A, leftB, ready_B, n):
                sB = sA + 1
                wait_slot(sA)
                pe.wait_ge(*ready_A)
                for e in range(2):
                    accumulate(sA, leftA, 0, e)
                wait_slot(sB)
                pe.wait_ge(*ready_B)
                for h in range(2):
                    accumulate_half(sB, leftB, 0, h).then_inc(acc_done, 1)
                for e in range(2):
                    last = accumulate(sA, leftA, 1, e)
                last.then_inc(slot_done, 1)
                accumulate_half(sB, leftB, 1, 0).then_inc(acc_done, 1)
                if n < 5:
                    transposes(n, 0)
                accumulate_half(sB, leftB, 1, 1).then_inc(slot_done, 1)

            def open_rows(s, n):
                for t in range(2):
                    for b in range(2):
                        if t == 0:
                            wait_slot(s + b)
                        last = project_rows(s + b, b, t, n, (lambda: transposes(n, 1)) if t == 0 and b == 1 else None)
                        if t == 1:
                            last.then_inc(slot_done, 1)

            def turn_opening(o):
                for b in range(2):
                    pe.wait_ge(opening_copied, 2 * o + b + 1)
                    for e in range(2):
                        for t in range(2):
                            last = pe.transpose(tr[b][:, 256 * e + P * t:256 * e + P * t + P],
                                                opening[:, b, 256 * t + P * e:256 * t + P * e + P], ident[:])
                    last.then_inc(opening_T, 1)

            def wide_after_opening(s, b, o):
                pe.wait_ge(opening_copied, 2 * o + b + 1)
                wait_slot(s)
                project(s, b, hidA, 0)
                if b == 0:
                    turn_opening(o)
                project(s, b, hidA, 1).then_inc(slot_done, 1)

            def wide_slot(s, b, hid, turn=None):
                wait_slot(s, turn)
                for e in range(2):
                    last = project(s, b, hid, e)
                last.then_inc(slot_done, 1)

            def deep_slot(s, left, first=False, turn=None):
                wait_slot(s, turn)
                for t in range(2):
                    for e in range(2):
                        last = accumulate(s, left, t, e, first=(first and e == 0))
                last.then_inc(slot_done, 1)

            def mix_pair(i):
                return [(mix_hi[:, 2 * i + e, :], mix_lo[:, 2 * i + e, :]) for e in range(2)]

            def act_pair(U):
                return [(act_hi[:, U % 2, e, :], act_lo[:, U % 2, e, :]) for e in range(2)]

            hidA, hidB = HID[0], HID[3]

            def gate_up(l, j, turn=None):
                s, U = gate_slot(l, j), l * UNITS + j
                pe.wait_ge(conv_op, after(4 * U, turn, 8))
                wide_slot(s, 0, hidA, turn)
                pe.wait_ge(act_full, after(U, turn, 2))
                wide_slot(s + 1, 1, hidA, turn)

            def down(l, j, turn=None):
                U = l * UNITS + j - 1
                pe.wait_ge(act_lo_ready, after(U + 1, turn, 2))
                deep_slot(gate_slot(l, j) + 2, act_pair(U), first=(j == 1), turn=turn)

            def ffn(l, n, next_n):
                open_rows(FFN[l], n)
                for b in range(2):
                    wide_after_opening(gate_slot(l, 1) + b, b, l + 1)
                pe.wait_ge(squared, step4(2 * l + 1, 1, 1))
                down(l, 1)
                with pe.Fori(0, TURNS) as turn:
                    for j in (2, 3):
                        gate_up(l, j, turn)
                        down(l, j, turn)
                j = UNITS - 1
                U = l * UNITS + j
                gate_up(l, j)
                finish(gate_slot(l, j) + 2, act_pair(U - 1), (act_lo_ready, U), act_pair(U), (act_lo_ready, U + 1), next_n)

            pe.wait_ge(consts, 1)
            def warm(count):
                for _ in range(count):
                    pe.matmul(acc[0][1][:, 0:P], ident[:], ident[:], start=True, stop=True)

            warm(4)
            pe.wait_ge(gain_in, 16)
            for h in range(2):
                pe.matmul(acc[1][h][:], ones[:], gain[0:1, 512 * h:512 * h + 512],
                          start=True, stop=True).then_inc(gain0_spread, 1)
            transposes(0, 0)
            warm(8)
            project_rows(0, 0, 0, 0, lambda: transposes(0, 1))
            project_rows(0, 0, 1, 0).then_inc(slot_done, 1)
            wait_slot(1)
            project_rows(1, 1, 0)
            project_rows(1, 1, 1).then_inc(slot_done, 1)
            pe.wait_ge(par_in, 16 * 5)
            R0, R1 = TAPS * KD, (TAPS + 1) * FT
            pe.transpose(acc[0][0][:, 0:R0], par_rows[0:R0, 0, :], ident[0:R0, 0:R0])
            for l in range(2):
                last = pe.transpose(acc[1][l][:, 0:R1], par_rows[0:R1, 1 + l, :], ident[0:R1, 0:R1])
            last.then_inc(par_T, 1)
            for b in range(2):
                wide_after_opening(A_IN + 2 + b, b, 0)
            for i in range(2, KD // 2):
                pe.wait_ge(c_copied, i)
                wide_slot(A_IN + 2 * i, 0, hidA)
                pe.wait_ge(cx_ready, i)
                wide_slot(A_IN + 2 * i + 1, 1, hidA)
            for i in range(KD // 2):
                pe.wait_ge(*[(c_copied, KD // 2), (cx_ready, KD // 2)][i] if i < 2 else (gated, i - 1))
                wide_slot(A_B + i, i % 2, hidA)
            pe.wait_ge(par_ready, 3)
            for i in range(KD // 2 - 2):
                pe.wait_ge(mix_lo_ready, i + 1)
                deep_slot(A_OUT + i, mix_pair(i), first=(i == 0))
            i = KD // 2 - 2
            finish(A_OUT + i, mix_pair(i), (mix_lo_ready, i + 1), mix_pair(i + 1), (mix_lo_ready, i + 2), 1)

            ffn(0, 1, 2)

            open_rows(V0, 2)
            for i in range(2, KD // 2):
                pe.wait_ge(v_lo_ready, i - 1)
                wait_slot(V0 + i)
                for t in range(2):
                    last = project_rows(V0 + i, i % 2, t)
                last.then_inc(slot_done, 1)
                transposes(3, i - 2)
            pe.wait_ge(v_lo_ready, 3)
            wide_slot(KQ0, 0, hidA)
            pe.wait_ge(v_lo_ready, 4)
            pe.wait_ge(h_lo_ready, step4(3, 1, 1))
            wide_slot(KQ0 + 1, 1, hidB)

            def scores(h):
                e, par = h % 2, h // 2 % 2
                pe.wait_ge(kq_lo_ready, 2 * (h // 2) + 2)
                if h >= 2:
                    pe.wait_ge(mix_lo_ready, KD // 2 + h - 1)
                K = (kq_hi[:, par, 0, 256 * e:256 * e + 256], kq_lo[:, par, 0, 256 * e:256 * e + 256])
                Q = (kq_hi[:, par, 1, 256 * e:256 * e + 256], kq_lo[:, par, 1, 256 * e:256 * e + 256])
                split_matmul(tr[e][:, 0:P], ([q[:, 0:P] for q in Q], [k[:, 0:P] for k in K]), True, True)
                split_matmul(tr[e][:, P:3 * P], ([q[:, P:2 * P] for q in Q], K), True, True).then_inc(scores_ready, 1)

            def transpose_probs(h):
                e = h % 2
                pe.wait_ge(probs_ready, 2 * h + 2)
                for c in range(3):
                    last = pe.transpose(tr[e][:, P * c:P * c + P], logits[:, e, P * c:P * c + P], ident[:])
                last.then_inc(probs_T, 1)

            def weigh(h):
                e = h % 2
                pe.wait_ge(pt_lo_ready, h + 1)
                V = [[v[:, t, P * h:P * h + P] for v in (v_hi, v_lo)] for t in range(2)]
                split_matmul(tr[e][:, 0:256], (V[0], (pt_hi[:, e, 0:256], pt_lo[:, e, 0:256])), True, False)
                split_matmul(tr[e][:, P:256], (V[1], (pt_hi[:, e, 256:384], pt_lo[:, e, 256:384])),
                             False, True).then_inc(heads_out, 1)

            for p in range(NH // 2 - 1):
                sK, sQ = KQ0 + 2 * p + 2, KQ0 + 2 * p + 3
                wait_slot(sK)
                pe.wait_ge(kq_lo_ready, 2 * p + 1)
                project(sK, 0, hidA, 0)
                scores(2 * p)
                scores(2 * p + 1)
                project(sK, 0, hidA, 1).then_inc(slot_done, 1)
                wait_slot(sQ)
                project(sQ, 1, hidB, 0)
                transpose_probs(2 * p)
                transpose_probs(2 * p + 1)
                project(sQ, 1, hidB, 1).then_inc(slot_done, 1)
                weigh(2 * p)
                weigh(2 * p + 1)
            p = NH // 2 - 1
            wait_slot(O0)
            pe.wait_ge(squared, step4(2, 1, 1))
            pe.wait_ge(mix_lo_ready, KD // 2 + 2)
            for e in range(2):
                accumulate(O0, mix_pair(0), 0, e, first=(e == 0))
            scores(2 * p)
            scores(2 * p + 1)
            for e in range(2):
                last = accumulate(O0, mix_pair(0), 1, e, first=(e == 0))
            last.then_inc(slot_done, 1)
            wait_slot(O0 + 1)
            pe.wait_ge(mix_lo_ready, KD // 2 + 4)
            for e in range(2):
                accumulate(O0 + 1, mix_pair(1), 0, e)
            transpose_probs(2 * p)
            transpose_probs(2 * p + 1)
            for e in range(2):
                last = accumulate(O0 + 1, mix_pair(1), 1, e)
            last.then_inc(slot_done, 1)
            weigh(2 * p)
            weigh(2 * p + 1)
            finish(O0 + 2, mix_pair(2), (mix_lo_ready, KD // 2 + 6), mix_pair(3), (mix_lo_ready, KD // 2 + 8), 4)

            ffn(1, 4, 5)


_INS = ["x", "norm_mix", "norm_ffn", "ffn_w_up", "ffn_conv", "ffn_conv_b", "ffn_w_down", "a_w_in", "a_conv",
        "a_w_out", "kv_norm", "w_kv", "b_w_q", "b_w_o", "final_norm"]


def kernel(**inputs):
    import numpy as np
    import concourse.bacc as bacc
    from concourse.bass_utils import run_bass_kernel_spmd

    nc = bacc.Bacc("TRN2", target_bir_lowering=False, num_devices=1)
    arrays, args = {}, []
    for name in _INS:
        a = np.ascontiguousarray(inputs[name])
        arrays[f"in_{name}"] = a
        args.append(nc.dram_tensor(f"in_{name}", a.shape, mybir.dt.from_np(a.dtype), kind="ExternalInput").ap())
    args.append(nc.dram_tensor("out", arrays["in_x"].shape, F32, kind="ExternalOutput").ap())
    build(nc, *args)
    return run_bass_kernel_spmd(nc, [arrays], core_ids=[0]).results[0]["out"]
```
